# Optimizing a Trainium2 kernel written in Bass

```python
import math
import jax, jax.numpy as jnp
from jax import lax
import numpy as np

D_MODEL = 1024
BATCH = 1
SEQ = 256
DEPTH = 2

CHUNK = 64
N_MIXERS = 2
N_POOL_LAYERS = (DEPTH + 1) // 2
N_ATTN_LAYERS = DEPTH // 2
RMS_EPS = 1e-6
POOL_WINDOWS = (2, 4, 8, 16)
POOL_GROUPS = len(POOL_WINDOWS)
POOL_GW = D_MODEL // POOL_GROUPS
N_HEADS = 8
HEAD_DIM = 64
D_ATTN = N_HEADS * 2 * HEAD_DIM
Q_BLOCK = 128
ATTN_SCALE = HEAD_DIM ** -0.5
SUBLN_EPS = 1e-5
NEG_INF = -1e30
N_GROUPS = 4
EXPERTS_PER_GROUP = 8
N_EXPERTS = N_GROUPS * EXPERTS_PER_GROUP
TOP_K = 2
D_EXPERT = 512
DISPATCH_BLOCK = 256

kernel_name = "hybrid_pool_diffattn_hiermoe"

def rms_norm(x, g, eps=RMS_EPS):
    xf = x.astype(jnp.float32)
    y = xf * lax.rsqrt(jnp.mean(xf * xf, axis=-1, keepdims=True) + eps)
    return (y * g.astype(jnp.float32)).astype(x.dtype)

def alibi_slopes(n_heads):
    return jnp.array([2.0 ** (-8.0 * (h + 1) / n_heads) for h in range(n_heads)], dtype=jnp.float32)

def pool_mixer(h, w, scale):
    B, S, D = h.shape
    hf = h.astype(jnp.float32)
    outs = []
    for gi, win in enumerate(POOL_WINDOWS):
        hg = hf[..., gi * POOL_GW:(gi + 1) * POOL_GW]
        cs = jnp.cumsum(hg, axis=1)
        lagged = jnp.pad(cs[:, :-win], ((0, 0), (win, 0), (0, 0)))
        cnt = jnp.minimum(jnp.arange(S) + 1, win).astype(jnp.float32)
        mix = (cs - lagged) / cnt[None, :, None] - hg
        outs.append(jnp.einsum('bsc,cd->bsd', mix.astype(h.dtype), w[gi]))
    return jnp.concatenate(outs, axis=-1) * scale

def diff_attention(h, wq, wk, wv, wo, lq1, lk1, lq2, lk2, subln_g, layer_idx):
    B, S, _ = h.shape
    nb = S // Q_BLOCK
    q = (h @ wq).reshape(B, S, N_HEADS, 2, HEAD_DIM)
    k = (h @ wk).reshape(B, S, N_HEADS, 2, HEAD_DIM)
    v = (h @ wv).reshape(B, S, N_HEADS, 2 * HEAD_DIM)
    lam_init = 0.8 - 0.6 * math.exp(-0.3 * layer_idx)
    f32 = jnp.float32
    lam = (jnp.exp(jnp.sum(lq1.astype(f32) * lk1.astype(f32)))
           - jnp.exp(jnp.sum(lq2.astype(f32) * lk2.astype(f32))) + lam_init)
    slopes = alibi_slopes(N_HEADS)
    sk = jnp.arange(S)
    k_chunk = sk // CHUNK
    q_blocks = q.reshape(B, nb, Q_BLOCK, N_HEADS, 2, HEAD_DIM).transpose(1, 0, 2, 3, 4, 5)

    def one_block(args):
        qb, bi = args
        tq = bi * Q_BLOCK + jnp.arange(Q_BLOCK)
        s = jnp.einsum('bqhcd,bkhcd->bhcqk', qb, k).astype(f32) * ATTN_SCALE
        dist = jnp.abs(tq[:, None] - sk[None, :]).astype(f32)
        allowed = k_chunk[None, :] <= (tq // CHUNK)[:, None]
        bias = jnp.where(allowed[None], -slopes[:, None, None] * dist[None], NEG_INF)
        p = jax.nn.softmax(s + bias[None, :, None], axis=-1)
        a = (p[:, :, 0] - lam * p[:, :, 1]).astype(v.dtype)
        return jnp.einsum('bhqk,bkhe->bqhe', a, v)

    o = lax.map(one_block, (q_blocks, jnp.arange(nb)))
    o = o.transpose(1, 0, 2, 3, 4).reshape(B, S, N_HEADS, 2 * HEAD_DIM)
    o = rms_norm(o, subln_g, SUBLN_EPS) * (1.0 - lam_init)
    return o.reshape(B, S, D_ATTN) @ wo

def hier_moe(h, wg, bg, we, be, w1, w3, w2):
    B, S, D = h.shape
    N = B * S
    xf = h.reshape(N, D)
    f32 = jnp.float32
    g_prob = jax.nn.softmax((xf @ wg).astype(f32) + bg.astype(f32), axis=-1)
    g_p, g_idx = lax.top_k(g_prob, 1)
    e_logits = ((xf @ we).astype(f32) + be.astype(f32)).reshape(N, N_GROUPS, EXPERTS_PER_GROUP)
    e_in = jnp.take_along_axis(e_logits, g_idx[:, :, None], axis=1)[:, 0]
    top_v, top_i = lax.top_k(e_in, TOP_K)
    gate = g_p * jax.nn.softmax(top_v, axis=-1)
    e_flat = (g_idx * EXPERTS_PER_GROUP + top_i).reshape(-1)
    tok_flat = jnp.repeat(jnp.arange(N), TOP_K)
    w_flat = gate.reshape(-1)
    NK = N * TOP_K
    order = jnp.argsort(e_flat)
    e_sorted = e_flat[order]
    tok_sorted = tok_flat[order]
    w_sorted = w_flat[order]
    counts = jnp.bincount(e_flat, length=N_EXPERTS)
    padded = ((counts + DISPATCH_BLOCK - 1) // DISPATCH_BLOCK) * DISPATCH_BLOCK
    pad_end = jnp.cumsum(padded)
    pad_start = pad_end - padded
    off_start = jnp.cumsum(counts) - counts
    dest = pad_start[e_sorted] + jnp.arange(NK) - off_start[e_sorted]
    n_slots = NK + N_EXPERTS * DISPATCH_BLOCK
    n_blocks = n_slots // DISPATCH_BLOCK
    slot_tok = jnp.zeros((n_slots,), jnp.int32).at[dest].set(tok_sorted)
    slot_w = jnp.zeros((n_slots,), h.dtype).at[dest].set(w_sorted.astype(h.dtype))
    block_expert = jnp.minimum(
        jnp.searchsorted(pad_end, jnp.arange(n_blocks) * DISPATCH_BLOCK, side='right'),
        N_EXPERTS - 1)
    xs = xf[slot_tok].reshape(n_blocks, DISPATCH_BLOCK, D)

    def expert_block(args):
        xb, e = args
        a = jax.nn.silu(xb @ w1[e]) * (xb @ w3[e])
        return a @ w2[e]

    ys = lax.map(expert_block, (xs, block_expert)).reshape(n_slots, D)
    y = jnp.zeros((N, D), h.dtype).at[slot_tok].add(ys * slot_w[:, None])
    return y.reshape(B, S, D)

def setup_inputs(seed: int = 0) -> dict:
    key = jax.random.key(seed)
    ks = jax.random.split(key, 24)
    f32 = jnp.float32
    D = D_MODEL

    def nrm(k, shape, scale):
        return jax.random.normal(k, shape, f32) * scale

    return {
        "x": nrm(ks[0], (BATCH, SEQ, D), 1.0),
        "norm_mix_g": 1.0 + nrm(ks[1], (DEPTH, D), 0.02),
        "norm_ffn_g": 1.0 + nrm(ks[2], (DEPTH, D), 0.02),
        "pool_w": nrm(ks[3], (N_POOL_LAYERS, POOL_GROUPS, POOL_GW, POOL_GW), POOL_GW ** -0.5),
        "pool_scale": 1.0 + nrm(ks[4], (N_POOL_LAYERS, D), 0.02),
        "attn_wq": nrm(ks[5], (N_ATTN_LAYERS, D, D_ATTN), D ** -0.5),
        "attn_wk": nrm(ks[6], (N_ATTN_LAYERS, D, D_ATTN), D ** -0.5),
        "attn_wv": nrm(ks[7], (N_ATTN_LAYERS, D, D_ATTN), D ** -0.5),
        "attn_wo": nrm(ks[8], (N_ATTN_LAYERS, D_ATTN, D), D_ATTN ** -0.5),
        "attn_lq1": nrm(ks[9], (N_ATTN_LAYERS, HEAD_DIM), 0.1),
        "attn_lk1": nrm(ks[10], (N_ATTN_LAYERS, HEAD_DIM), 0.1),
        "attn_lq2": nrm(ks[11], (N_ATTN_LAYERS, HEAD_DIM), 0.1),
        "attn_lk2": nrm(ks[12], (N_ATTN_LAYERS, HEAD_DIM), 0.1),
        "attn_subln_g": 1.0 + nrm(ks[13], (N_ATTN_LAYERS, 2 * HEAD_DIM), 0.02),
        "moe_wg": nrm(ks[14], (DEPTH, D, N_GROUPS), D ** -0.5),
        "moe_bg": nrm(ks[15], (DEPTH, N_GROUPS), 0.01),
        "moe_we": nrm(ks[16], (DEPTH, D, N_EXPERTS), D ** -0.5),
        "moe_be": nrm(ks[17], (DEPTH, N_EXPERTS), 0.01),
        "moe_w1": nrm(ks[18], (DEPTH, N_EXPERTS, D, D_EXPERT), D ** -0.5),
        "moe_w3": nrm(ks[19], (DEPTH, N_EXPERTS, D, D_EXPERT), D ** -0.5),
        "moe_w2": nrm(ks[20], (DEPTH, N_EXPERTS, D_EXPERT, D), D_EXPERT ** -0.5),
        "final_g": 1.0 + nrm(ks[21], (D,), 0.02),
    }

def reference(x, norm_mix_g, norm_ffn_g, pool_w, pool_scale, attn_wq, attn_wk, attn_wv, attn_wo,
              attn_lq1, attn_lk1, attn_lq2, attn_lk2, attn_subln_g, moe_wg, moe_bg, moe_we, moe_be,
              moe_w1, moe_w3, moe_w2, final_g):
    for i in range(DEPTH):
        h = rms_norm(x, norm_mix_g[i])
        j = i // N_MIXERS
        if i % N_MIXERS == 0:
            x = x + pool_mixer(h, pool_w[j], pool_scale[j])
        else:
            x = x + diff_attention(h, attn_wq[j], attn_wk[j], attn_wv[j], attn_wo[j],
                                   attn_lq1[j], attn_lk1[j], attn_lq2[j], attn_lk2[j],
                                   attn_subln_g[j], i)
        h = rms_norm(x, norm_ffn_g[i])
        x = x + hier_moe(h, moe_wg[i], moe_bg[i], moe_we[i], moe_be[i],
                         moe_w1[i], moe_w3[i], moe_w2[i])
    return rms_norm(x, final_g)


_drawn_inputs = setup_inputs


def setup_inputs(seed=0):
    import zlib

    import numpy as np

    out = dict(_drawn_inputs(seed))
    spreads = {}
    factors = {'attn_lq1': 5.111,
     'attn_lk1': 8.0,
     'attn_subln_g': 10.373,
     'moe_bg': 9.282,
     'moe_be': 3.298,
     'final_g': 7.547,
     'attn_lq2': 8.0,
     'attn_lk2': 8.0}
    for name, (base, spread) in spreads.items():
        noise = np.random.default_rng([zlib.crc32(name.encode()), seed]).standard_normal(out[name].shape)
        drawn = base * np.exp(spread * noise) if base else spread * noise
        out[name] = __import__('jax').numpy.asarray(drawn.astype(out[name].dtype))
    for name, factor in factors.items():
        out[name] = (out[name] * factor).astype(out[name].dtype)
    return out
```

```python
import math
from contextlib import ExitStack

import numpy as np

import concourse.bass as bass
from concourse import mybir

F32 = mybir.dt.float32
I32 = mybir.dt.int32
ALU = mybir.AluOpType
ACT = mybir.ActivationFunctionType
AX = mybir.AxisListType.X

P = 128
S, D = 256, 1024
TH = S // P
KT = D // P
NH, HD = 8, 64
NG, EPG = 4, 8
NE = NG * EPG
F = 512
JT = F // P
SB = 32
NB = 2
CAP = SB * NB
PASSES = S // CAP
E4 = P // SB
GPB = 2
BODY = GPB * E4
ITERS = NE // BODY
NGRP = NE // E4
RING = 8
CH = 4096
CPE = 3
ACH = 8
WINDOWS = (2, 4, 8, 16)
RMS_EPS, SUB_EPS = 1e-6, 1e-5
BIG = 1024.0
PEN = 1e30
LAM_INIT = 0.8 - 0.6 * math.exp(-0.3)
LW = P + S
NR = NG + NE
assert (CPE * NE) % RING == 0 and ACH % RING == 0 and (CPE * BODY) % RING == 0

C_ID, C_U, C_ONE, C_DIST = 0, P, 2 * P, 3 * P
C_IOTA = C_DIST + LW
C_BAND = C_IOTA + CAP
BW = S + P
C_ALL = C_BAND + len(WINDOWS) * BW


def shape_constants():
    c = np.zeros((P, C_ALL), np.float32)
    i = np.arange(P)
    c[:, C_ID:C_ID + P] = np.eye(P)
    c[:, C_U:C_U + P] = i[:, None] < i[None, :]
    c[:, C_ONE:C_ONE + P] = 1.0
    for half, at, keys in ((0, 0, P), (1, P, S)):
        q, k = i[:, None] + half * P, np.arange(keys)[None, :]
        c[:, C_DIST + at:C_DIST + at + keys] = np.where(k // 64 <= q // 64, np.abs(q - k), 1e33)
    c[:, C_IOTA:C_IOTA + CAP] = np.arange(CAP)
    for g, win in enumerate(WINDOWS):
        t = np.arange(S)
        lag = t[None, :] - t[:, None]
        band = ((lag >= 0) & (lag < win)) / np.minimum(t + 1, win)[None, :] - (lag == 0)
        at = C_BAND + g * BW
        c[:, at:at + S] = band[:P]
        c[:, at + S:at + BW] = band[P:, P:]
    return c


def build(nc, x, norm_mix_g, norm_ffn_g, pool_w, pool_scale, wq, wk, wv, wo, lq1, lk1, lq2, lk2, subln_g,
          moe_wg, moe_bg, moe_we, moe_be, moe_w1, moe_w3, moe_w2, final_g, consts, out):
    with ExitStack() as ctx:
        def sb(name, shape, dt=F32):
            return ctx.enter_context(nc.sbuf_tensor(name, shape, dt))

        def sem(name):
            return ctx.enter_context(nc.semaphore(name))

        ring = sb("ring", [P, RING, CH])
        x_sb = sb("x_sb", [P, TH, D])
        h_sb = sb("h_sb", [P, TH, D])
        hT = sb("hT", [P, KT, S])
        gain = sb("gain", [P, 2, D])
        cst = sb("cst", [P, C_BAND])
        work = sb("work", [P, 6144])
        work2 = sb("work2", [P, 2304])
        wr = sb("wr", [P, 2, KT, NR])
        rb = sb("rb", [P, 2, NR])
        lam4 = sb("lam4", [P, 4, HD])
        subg = sb("subg", [P, 2 * HD])
        R = sb("R", [P, TH, NE])
        W = sb("W", [P, TH, NE])
        A = sb("A", [P, TH, NE])
        small = sb("small", [P, 1024])
        cnt = sb("cnt", [P, NGRP + 1], I32)
        ident, upper, ones = (cst[:, c:c + P] for c in (C_ID, C_U, C_ONE))
        dist = cst[:, C_DIST:C_DIST + LW]
        iota = cst[:, C_IOTA:C_IOTA + CAP]

        ssq = small[:, 0:2]
        zero = small[:, 64:64 + P]
        mean_x, rstd_x, mean_o, rstd_o = small[:, 2:4], small[:, 4:6], small[:, 780:788], small[:, 788:796]

        band = work[:, 0:len(WINDOWS) * BW]
        pw = work[:, 1536:1536 + 2048].rearrange("p (g c d) -> p g c d", g=4, c=2)
        mixT = work[:, 3584:3584 + 2048].rearrange("p (m s) -> p m s", m=KT)
        qT = work[:, 0:2048].rearrange("p (h s) -> p h s", h=NH)
        kT = work[:, 2048:4096].rearrange("p (h s) -> p h s", h=NH)
        v_sb = work[:, 4096:6144].rearrange("p (t n) -> p t n", t=TH)
        prob = work2[:, 0:4 * LW].rearrange("p (b c w) -> p b c w", b=2, c=2)
        aT = work2[:, 4 * LW:6 * LW].rearrange("p (b w) -> p b w", b=2)
        xg = work[:, 0:512].rearrange("p (k c) -> p k c", k=KT)
        sg = work[:, 512:1536].rearrange("p (m b f) -> p m b f", m=4, b=NB)
        act = work[:, 1536:1792].rearrange("p (b f) -> p b f", b=NB)
        actT = work[:, 1792:2048].rearrange("p (b r) -> p b r", b=NB)
        y = work[:, 2048:4096].rearrange("p (b n) -> p b n", b=NB)
        onehot = work2[:, 0:512].rearrange("p (t b e s) -> p t b e s", t=TH, b=NB, e=E4)
        gated = work2[:, 512:1024].rearrange("p (t b e s) -> p t b e s", t=TH, b=NB, e=E4)
        gateT = work2[:, 1024:1536].rearrange("p (b s) -> p b s", b=NB)

        ps = ctx.enter_context(nc.psum_tensor("ps", [P, 8, 512], F32))
        acc = ps[:, 0:4, :].rearrange("p (t n) w -> p t n w", t=TH)
        xg_ps = ps[:, 4, :].rearrange("p (k c) -> p k c", k=KT)
        gu_ps = ps[:, 5, :].rearrange("p (b m f) -> p b m f", b=NB, m=2)
        gt_ps = ps[:, 5, :].rearrange("p (b s) -> p b s", b=NB)
        y_ps = ps[:, 6, :].rearrange("p (b n) -> p b n", b=NB)
        at_ps = ps[:, 7, 0:256].rearrange("p (b r) -> p b r", b=NB)

        loaded = [sem(f"loaded{i}") for i in range(RING)]
        s_w = sem("s_w")
        s_x, s_c, s_band, s_pw, s_wr, s_lam = (sem(n) for n in ("s_x", "s_c", "s_band", "s_pw", "s_wr", "s_lam"))
        gain_in = [sem("gain_in0"), sem("gain_in1")]
        s_out = sem("s_out")
        s_ssq = sem("s_ssq")
        s_x2 = sem("s_x2")
        s_h = sem("s_h")
        s_mix, s_po = sem("s_mix"), sem("s_po")
        s_mixT = [sem("s_mixT_v"), sem("s_mixT_a")]
        s_oTc = [sem("s_oTc_v"), sem("s_oTc_a")]
        s_tr, s_hT = sem("s_tr"), sem("s_hT")
        s_lg, s_A, s_rk, s_route = sem("s_lg"), sem("s_A"), sem("s_rk"), sem("s_route")
        s_dg, s_eg = sem("s_dg"), sem("s_eg")
        s_v = sem("s_v")
        s_a = sem("s_a")
        s_mean, s_root = sem("s_mean"), sem("s_root")
        s_z = sem("s_z")
        s_q, s_qc, s_kc, s_vp, s_vs = sem("s_q"), sem("s_qc"), sem("s_kc"), sem("s_vp"), sem("s_vs")
        s_S, s_L, s_ex, s_p = sem("s_S"), sem("s_L"), sem("s_ex"), sem("s_p")
        s_m = sem("s_m")
        s_aT, s_aTc, s_o, s_osq, s_os = sem("s_aT"), sem("s_aTc"), sem("s_o"), sem("s_osq"), sem("s_os")
        s_oT, s_wo = sem("s_oT"), sem("s_wo")
        s_ls, s_le = sem("s_ls"), sem("s_le")

        STEPS = ("onehot", "gated", "xg", "xgc", "half", "gu", "exp", "den", "sig", "gh", "act", "at", "atc", "y", "yc",
                 "gt", "gtc", "sc", "shift", "passed", "wl0", "wl1", "wl2")

        def moe_sems(name):
            return {k: sem(f"{name}_{k}") for k in STEPS}

        main = moe_sems("m")
        more = [moe_sems("p0"), moe_sems("p1")]

        def use_before(layer):
            return layer * (CPE * NE + ACH) // RING

        def chunk_parts(layer, e, j):
            if j < 2:
                return [(m * 2048, w[layer, e, :, :].rearrange("(p k) n -> p k n", k=KT)[:, 4 * j:4 * j + 4, :])
                        for m, w in ((0, moe_w1), (1, moe_w3))]
            w = moe_w2[layer, e, :, :].rearrange("(j p) n -> p j n", p=P)
            return [(m * 2048, w[:, 2 * m:2 * m + 2, :]) for m in range(2)]

        def attn_parts(c):
            w = (wq, wk, wv, wo)[c // 2]
            if c < 6:
                w = w[0].rearrange("(p k) n -> p k n", k=KT)
            else:
                w = w[0].rearrange("(k p) n -> p k n", p=P)
            at = 4 * (c % 2)
            return [(m * 2048, w[:, at + 2 * m:at + 2 * m + 2, :]) for m in range(2)]

        def view(src):
            return src.shape[1], src.shape[2]

        block = ctx.enter_context(nc.Block())

        @block.sync
        def _(sp):
            def load(slot, parts, signal):
                for at, src in parts:
                    k, n = view(src)
                    sp.dma_start(ring[:, slot, at:at + k * n].rearrange("p (k n) -> p k n", k=k), src) \
                      .then_inc(signal, 16)

            sp.dma_start(x_sb[:, :, :], x[0].rearrange("(t p) d -> p t d", p=P)).then_inc(s_x, 16)
            sp.dma_start(cst[:, :], consts[:, 0:C_BAND]).then_inc(s_c, 16)
            sp.dma_start(band, consts[:, C_BAND:C_ALL]).then_inc(s_band, 16)
            sp.dma_start(pw, pool_w[0].rearrange("g (c p) d -> p g c d", p=P)).then_inc(s_pw, 16)
            used = (main["half"], main["gu"], main["y"])
            attn_used = ((s_w, 1), (s_q, 1), (s_w, 2), (s_q, 2), (s_w, 3), (s_vp, 1), (s_w, 4), (s_wo, 1))
            for layer in range(2):
                for c in range(RING):
                    if layer == 1:
                        sp.wait_ge(*attn_used[c])
                    load(c, chunk_parts(layer, c // CPE, c % CPE), loaded[c])
                steady = CPE * BODY

                def stream(it, c):
                    e, j = divmod(c - RING, CPE)
                    sp.wait_ge(used[j], it * BODY + (layer * NE + e + 1))
                    load(c % RING, chunk_parts(layer, it * BODY + c // CPE, c % CPE), loaded[c % RING])

                with sp.Fori(0, ITERS - 1) as it:
                    for c in range(RING, RING + steady):
                        stream(it, c)
                for c in range(RING, steady):
                    stream(ITERS - 1, c)
                fb = more[layer]
                sp.wait_ge(s_route, layer + 1)
                most = sp.value_load(cnt[0:1, NGRP:NGRP + 1], min_val=0, max_val=S)
                with sp.If(most > CAP):
                    sp.wait_ge(main["y"], NE * (layer + 1))
                    with sp.Fori(0, PASSES - 1) as m:
                        with sp.If(most > CAP * m + CAP):
                            with sp.Fori(0, NE) as e:
                                n = m * NE + e
                                for j in range(CPE):
                                    load(j, chunk_parts(layer, e, j), fb[f"wl{j}"])
                                sp.wait_ge(fb["y"], n + 1)
                                sp.sem_inc(fb["passed"], 1)
                if layer == 0:
                    for c in range(ACH):
                        e, j = divmod(CPE * NE - RING + c, CPE)
                        sp.wait_ge(used[j], e + 1)
                        load(c, attn_parts(c), loaded[c])
            sp.wait_ge(s_h, 5)
            sp.dma_start(out[0].rearrange("(t p) d -> p t d", p=P), h_sb[:, :, :]).then_inc(s_out, 16)
            sp.wait_ge(s_out, 16)

        @block.gpsimd
        def _(pool):
            def row(dst, src):
                return pool.dma_start(dst, src.to_broadcast([P] + list(src.shape[1:])))

            row(gain[:, 0, :], norm_mix_g[0:1, :]).then_inc(gain_in[0], 16)
            row(gain[:, 1, :], pool_scale[0:1, :]).then_inc(gain_in[1], 16)
            for layer in range(2):
                pool.dma_start(wr[:, layer, :, 0:NG], moe_wg[layer].rearrange("(p k) n -> p k n", k=KT)).then_inc(s_wr, 16)
                pool.dma_start(wr[:, layer, :, NG:NR], moe_we[layer].rearrange("(p k) n -> p k n", k=KT)).then_inc(s_wr, 16)
                row(rb[:, layer, 0:NG], moe_bg[layer:layer + 1, :]).then_inc(s_wr, 16)
                row(rb[:, layer, NG:NR], moe_be[layer:layer + 1, :]).then_inc(s_wr, 16)
            for i, w in enumerate((lq1, lk1, lq2, lk2)):
                row(lam4[:, i, :], w[0:1, :]).then_inc(s_lam, 16)
            row(subg[:, :], subln_g[0:1, :]).then_inc(s_lam, 16)
            pool.wait_ge(s_h, 1)
            row(gain[:, 0, :], norm_ffn_g[0:1, :]).then_inc(gain_in[0], 16)
            pool.wait_ge(s_x2, 1)
            row(gain[:, 1, :], norm_mix_g[1:2, :]).then_inc(gain_in[1], 16)
            pool.wait_ge(s_h, 2)
            row(gain[:, 0, :], norm_ffn_g[1:2, :]).then_inc(gain_in[0], 16)
            pool.wait_ge(s_h, 3)
            row(gain[:, 1, :], final_g.rearrange("(a d) -> a d", a=1)).then_inc(gain_in[1], 16)

        @block.tensor
        def _(pe):
            def transposes(count):
                for k in range(KT):
                    for t in range(TH):
                        mm = pe.transpose(ps[:, k // 2, (k % 2) * S + t * P:(k % 2) * S + t * P + P],
                                          h_sb[:, t, k * P:(k + 1) * P], ident)
                    if k % 2 == 1:
                        mm.then_inc(s_tr, 1)

            def route(layer, hT_count):
                pe.wait_ge(s_hT, hT_count)
                if layer == 0:
                    pe.wait_ge(s_wr, 128)
                for t in range(TH):
                    for k in range(KT):
                        mm = pe.matmul(ps[:, 5, t * 64:t * 64 + NR], hT[:, k, t * P:(t + 1) * P],
                                       wr[:, layer, k, :], start=(k == 0), stop=(k == KT - 1))
                mm.then_inc(s_lg, 1)
                pe.wait_ge(s_z, 1)
                for b in range(4):
                    pe.matmul(ps[:, b, :], zero, h_sb[:, 0, 0:512], start=True, stop=True)
                pe.wait_ge(s_A, layer + 1)
                pe.matmul(ps[:, 6, 0:NE], upper, A[:, 0, :], start=True, stop=True)
                pe.matmul(ps[:, 6, NE:2 * NE], ones, A[:, 0, :], start=True, stop=False)
                pe.matmul(ps[:, 6, NE:2 * NE], upper, A[:, 1, :], start=False, stop=True)
                pe.matmul(ps[:, 6, 2 * NE:3 * NE], ones, A[:, 0, :], start=True, stop=False)
                pe.matmul(ps[:, 6, 2 * NE:3 * NE], ones, A[:, 1, :], start=False, stop=True).then_inc(s_rk, 1)

            def group(s, g, blocks, chunk):
                def gather(k):
                    for kt in range(KT):
                        for t in range(TH):
                            mm = pe.matmul(xg_ps[:, kt, :], h_sb[:, t, kt * P:(kt + 1) * P],
                                           onehot[:, t, :, k, :], start=(t == 0), stop=(t == TH - 1))
                    mm.then_inc(s["xg"], 1)

                pe.wait_ge(s["onehot"], g + 1)
                gather(0)
                for k in range(E4):
                    n1 = g * E4 + k + 1
                    pe.wait_ge(s["xgc"], n1)
                    for half in range(2):
                        w = ring[:, chunk(k, half), :].rearrange("p (m k n) -> p m k n", m=2, k=4)
                        for b in reversed(range(blocks)):
                            for q in range(4):
                                for j in range(JT):
                                    mm = pe.matmul(gu_ps[SB * j:SB * (j + 1), b, :, :],
                                                   xg[:, 4 * half + q, SB * b:SB * (b + 1)],
                                                   w[:, :, q, P * j:P * (j + 1)],
                                                   start=(half == 0 and q == 0 and b == blocks - 1),
                                                   stop=(half == 1 and q == 3), skip_group_check=True)
                        mm.then_inc(s["half"] if half == 0 else s["gu"], 1)
                    if k + 1 < E4:
                        gather(k + 1)
                    pe.wait_ge(s["act"], n1)
                    for b in range(blocks):
                        mm = pe.transpose(at_ps[:, b, :], act[:, b, :], ident)
                    mm.then_inc(s["at"], 1)
                    if k == E4 - 1:
                        pe.wait_ge(s["gated"], g + 1)
                        for b in range(NB):
                            for t in range(TH):
                                mm = pe.transpose(gt_ps[:, b, t * P:(t + 1) * P],
                                                  gated[:, t, b, :, :].rearrange("p e s -> p (e s)"), ident)
                        mm.then_inc(s["gt"], 1)
                    pe.wait_ge(s["atc"], n1)
                    if k > 0:
                        pe.wait_ge(s["yc"], n1 - 1)
                    w = ring[:, chunk(k, 2), :].rearrange("p (j n) -> p j n", j=JT)
                    for b in range(blocks):
                        for j in range(JT):
                            for i in range(4):
                                mm = pe.matmul(y_ps[SB * i:SB * (i + 1), b, :], actT[:, b, SB * j:SB * (j + 1)],
                                               w[:, j, 256 * i:256 * (i + 1)], start=(j == 0), stop=(j == JT - 1))
                    mm.then_inc(s["y"], 1)
                pe.wait_ge(s["gtc"], g + 1)
                pe.wait_ge(s["yc"], g * E4 + E4)
                for b in range(blocks):
                    for t in range(TH):
                        for i in range(2):
                            mm = pe.matmul(acc[:, t, i, :], gateT[:, b, t * P:(t + 1) * P],
                                           y[:, b, 512 * i:512 * (i + 1)], start=False, stop=False,
                                           skip_group_check=True)
                mm.then_inc(s["sc"], 1)

            def experts(layer):
                u0 = use_before(layer)
                pe.wait_ge(s_route, layer + 1)
                with pe.Fori(0, ITERS) as it:
                    for gg in range(GPB):
                        g = it * GPB + (layer * NGRP + gg)
                        fullest = pe.value_load(cnt[0:1, bass.ds(it * GPB + gg, 1)], min_val=0, max_val=S)

                        def chunk(k, j, gg=gg):
                            c = CPE * (gg * E4 + k) + j
                            pe.wait_ge(loaded[c % RING], (it * (CPE * BODY // RING) + (u0 + c // RING + 1)) * 32)
                            return c % RING

                        with pe.If(fullest > SB):
                            group(main, g, NB, chunk)
                        with pe.Else():
                            group(main, g, 1, chunk)
                fb = more[layer]
                most = pe.value_load(cnt[0:1, NGRP:NGRP + 1], min_val=0, max_val=S)
                with pe.If(most > CAP):
                    with pe.Fori(0, PASSES - 1) as m:
                        with pe.If(most > CAP * m + CAP):
                            with pe.Fori(0, NGRP) as gg:
                                g = m * NGRP + gg

                                def chunk(k, j):
                                    pe.wait_ge(fb[f"wl{j}"], (g * E4 + (k + 1)) * 32)
                                    return j

                                group(fb, g, NB, chunk)

            pe.wait_ge(s_h, 1)
            pe.wait_ge(s_band, 16)
            for m in range(KT):
                at = (m // 2) * BW
                o = ps[:, m // 2, (m % 2) * S:(m % 2 + 1) * S]
                pe.matmul(o, h_sb[:, 0, m * P:(m + 1) * P], band[:, at:at + S], start=True, stop=False)
                mm = pe.matmul(o[:, P:S], h_sb[:, 1, m * P:(m + 1) * P], band[:, at + S:at + BW], start=False, stop=True)
                if m % 2 == 1:
                    mm.then_inc(s_mix, 1)
            pe.wait_ge(s_pw, 16)
            for g in range(4):
                pe.wait_ge(s_mixT[g % 2], g // 2 + 1)
                for t in range(TH):
                    for c in range(2):
                        mm = pe.matmul(ps[:, 4 + 2 * t + g // 2, (g % 2) * S:(g % 2 + 1) * S],
                                       mixT[:, 2 * g + c, t * P:(t + 1) * P], pw[:, g, c, :],
                                       start=(c == 0), stop=(c == 1))
            mm.then_inc(s_po, 1)
            pe.wait_ge(s_c, 16)
            pe.wait_ge(s_h, 2)
            transposes(0)
            route(0, 4)
            experts(0)

            pe.wait_ge(s_h, 3)
            transposes(1)
            pe.wait_ge(s_hT, 8)
            for c, name in ((0, s_q), (2, s_q)):
                if c == 0:
                    u = CPE * NE // RING + 1
                for kt in range(KT):
                    if kt % 4 == 0:
                        pe.wait_ge(loaded[c + kt // 4], 32 * u)
                    w = ring[:, c + kt // 4, :].rearrange("p (k n) -> p k n", k=4)
                    for h in range(NH):
                        mm = pe.matmul(ps[:, 2 * c + h // 2, (h % 2) * S:(h % 2 + 1) * S],
                                       w[:, kt % 4, h * P:(h + 1) * P], hT[:, kt, :],
                                       start=(kt == 0 and h % 2 == 0), stop=(kt == KT - 1), skip_group_check=True)
                    if kt == 3:
                        mm.then_inc(s_w, 1)
                mm.then_inc(name, 1)

            def scores(h):
                b = 4 + 2 * (h % 2)
                if h >= 2:
                    pe.wait_ge(s_L, 2 * (h - 1))
                for c in range(2):
                    r = slice(HD * c, HD * (c + 1))
                    pe.matmul(ps[:, b + c, 0:P], qT[r, h, 0:P], kT[r, h, 0:P], start=True, stop=True)
                    mm = pe.matmul(ps[:, b + c, P:LW], qT[r, h, P:S], kT[r, h, :], start=True, stop=True)
                mm.then_inc(s_S, 1)

            pe.wait_ge(s_qc, 4)
            for kt in range(KT):
                if kt % 4 == 0:
                    pe.wait_ge(loaded[4 + kt // 4], 32 * u)
                w = ring[:, 4 + kt // 4, :].rearrange("p (k n) -> p k n", k=4)
                for t in range(TH):
                    for i in range(2):
                        mm = pe.matmul(ps[:, 2 * t + i, :], hT[:, kt, t * P:(t + 1) * P],
                                       w[:, kt % 4, 512 * i:512 * (i + 1)], start=(kt == 0), stop=(kt == KT - 1))
                if kt == 3:
                    mm.then_inc(s_w, 1)
                if kt == KT - 1:
                    mm.then_inc(s_vp, 1)
                if kt == 0:
                    pe.wait_ge(s_kc, 4)
                scores(kt)
            pe.wait_ge(s_vs, 4)
            for h in range(NH):
                pe.wait_ge(s_p, h + 1)
                if h >= 2:
                    pe.wait_ge(s_aTc, h - 1)
                if h == 0:
                    pe.wait_ge(s_L, 2 * NH)
                bank = ps[:, 6 + h % 2, :]
                pe.transpose(bank[:, 0:P], kT[:, h, 0:P], ident)
                pe.transpose(bank[:, P:2 * P], qT[:, h, 0:P], ident)
                pe.transpose(bank[:, 2 * P:3 * P], qT[:, h, P:S], ident).then_inc(s_aT, 1)
                pe.wait_ge(s_aTc, h + 1)
                e = slice(h * P, (h + 1) * P)
                col = slice((h % 4) * P, (h % 4 + 1) * P)
                pe.matmul(ps[:, h // 4, col], aT[:, h % 2, 0:P], v_sb[:, 0, e], start=True, stop=True)
                pe.matmul(ps[:, 2 + h // 4, col], aT[:, h % 2, P:2 * P], v_sb[:, 0, e], start=True, stop=False)
                mm = pe.matmul(ps[:, 2 + h // 4, col], aT[:, h % 2, 2 * P:3 * P], v_sb[:, 1, e], start=False, stop=True)
                mm.then_inc(s_o, 1)
            for h in range(NH):
                if h % 4 == 0:
                    pe.wait_ge(s_os, h // 4 + 1)
                for t in range(TH):
                    mm = pe.transpose(ps[:, 4 + h // 2, (h % 2) * S + t * P:(h % 2) * S + (t + 1) * P],
                                      h_sb[:, t, h * P:(h + 1) * P], ident)
                if h % 2 == 1:
                    mm.then_inc(s_oT, 1)
            for h in range(NH):
                if h % 4 == 0:
                    pe.wait_ge(loaded[6 + h // 4], 32 * u)
                if h % 2 == 0:
                    pe.wait_ge(s_oTc[1 - h // 2 % 2], h // 4 + 1)
                w = ring[:, 6 + h // 4, :].rearrange("p (k n) -> p k n", k=4)
                for t in range(TH):
                    for i in range(2):
                        mm = pe.matmul(ps[:, 2 * t + i, :], hT[:, h, t * P:(t + 1) * P],
                                       w[:, h % 4, 512 * i:512 * (i + 1)], start=(h == 0), stop=(h == NH - 1))
                if h == 3:
                    mm.then_inc(s_w, 1)
            mm.then_inc(s_wo, 1)

            pe.wait_ge(s_h, 4)
            transposes(2)
            route(1, 12)
            experts(1)

        junk_a = work2[:, 0:D]

        @block.scalar
        def _(act_e):
            chain = [0]

            def root(number, mean):
                act_e.wait_ge(s_mean, number)
                act_e.activation(mean, mean, ACT.Sqrt).then_inc(s_root, 1)

            def squares(count):
                for t in range(TH):
                    chain[0] += 1
                    act_e.activation(junk_a, x_sb[:, t, :], ACT.Square, accum_out=ssq[:, t:t + 1]).then_inc(s_a, 1)
                    if t == 0:
                        act_e.wait_ge(s_a, chain[0])
                act_e.wait_ge(s_a, chain[0])
                act_e.sem_inc(s_ssq, 1)
                root(count + (1 if count < 3 else 3), mean_x)

            def copy_hT(first):
                for b in (0, 2):
                    act_e.wait_ge(s_tr, first + b + 1)
                    act_e.copy(hT[:, 2 * b:2 * b + 2, :], ps[:, b, :].rearrange("p (k s) -> p k s", k=2)).then_inc(s_hT, 1)

            def group(s, g):
                def gathered(k):
                    act_e.wait_ge(s["xg"], g * E4 + (k + 1))
                    act_e.copy(xg[:, :, :], xg_ps).then_inc(s["xgc"], 1)

                gathered(0)
                for k in range(E4):
                    n1 = g * E4 + (k + 1)
                    act_e.wait_ge(s["gu"], n1)
                    act_e.activation(sg[:, 0, :, :], gu_ps[:, :, 0, :], ACT.Exp, scale=-1.0).then_inc(s["exp"], 1)
                    if k + 1 < E4:
                        gathered(k + 1)
                    act_e.wait_ge(s["y"], n1)
                    for i in range(4):
                        ins = act_e.copy(y[SB * k:SB * (k + 1), :, 256 * i:256 * (i + 1)],
                                         y_ps[SB * i:SB * (i + 1), :, :])
                    ins.then_inc(s["yc"], 1)

            def experts(layer):
                act_e.wait_ge(s_route, layer + 1)
                with act_e.Fori(0, NGRP) as g:
                    group(main, g + layer * NGRP)
                fb = more[layer]
                most = act_e.value_load(cnt[0:1, NGRP:NGRP + 1], min_val=0, max_val=S)
                with act_e.If(most > CAP):
                    with act_e.Fori(0, PASSES - 1) as m:
                        with act_e.If(most > CAP * m + CAP):
                            with act_e.Fori(0, NGRP) as g:
                                group(fb, m * NGRP + g)

            def route(layer):
                act_e.wait_ge(s_dg, 2 * layer + 1)
                act_e.activation(small[:, 400:408], small[:, 408:416], ACT.Exp).then_inc(s_eg, 1)
                act_e.wait_ge(s_dg, 2 * layer + 2)
                act_e.activation(small[:, 416:418], small[:, 418:420], ACT.Exp).then_inc(s_eg, 1)

            act_e.wait_ge(s_x, 16)
            squares(0)
            for g in (1, 3):
                act_e.wait_ge(s_mix, g + 1)
                act_e.copy(mixT[:, 2 * g:2 * g + 2, :], ps[:, g, :].rearrange("p (m s) -> p m s", m=2))\
                     .then_inc(s_mixT[1], 1)
            act_e.wait_ge(s_x2, 1)
            squares(1)
            copy_hT(0)
            route(0)
            experts(0)

            act_e.wait_ge(s_x2, 2)
            squares(2)
            act_e.wait_ge(s_ls, 1)
            act_e.activation(small[:, 434:436], small[:, 432:434], ACT.Exp).then_inc(s_le, 1)
            copy_hT(4)
            act_e.wait_ge(s_q, 1)
            for b in (0, 2):
                act_e.mul(qT[:, 2 * b:2 * b + 2, :], ps[:, b, :].rearrange("p (h s) -> p h s", h=2), HD ** -0.5)\
                     .then_inc(s_qc, 1)
            act_e.wait_ge(s_q, 2)
            for b in (0, 2):
                act_e.copy(kT[:, 2 * b:2 * b + 2, :], ps[:, 4 + b, :].rearrange("p (h s) -> p h s", h=2))\
                     .then_inc(s_kc, 1)

            def attention_exp(h):
                act_e.wait_ge(s_m, 4 * (h + 1))
                for c in range(2):
                    for t, cols in ((0, slice(0, P)), (1, slice(P, LW))):
                        at = 440 + 8 * (h % 2) + 2 * c + t
                        ins = act_e.activation(prob[:, h % 2, c, cols], prob[:, h % 2, c, cols], ACT.Exp,
                                               bias=small[:, at:at + 1], accum_out=small[:, at + 4:at + 5])
                        ins.then_inc(s_ex, 1)

            for h in range(NH):
                attention_exp(h)
            act_e.wait_ge(s_vp, 1)
            for b in (0, 2):
                act_e.copy(v_sb[:, b // 2, 0:512], ps[:, b, :]).then_inc(s_vs, 1)
            for h in range(NH):
                act_e.wait_ge(s_aT, h + 1)
                act_e.copy(aT[:, h % 2, :], ps[:, 6 + h % 2, 0:LW]).then_inc(s_aTc, 1)
                if h % 4 == 3:
                    act_e.wait_ge(s_o, h + 1)
                    for hh in range(h - 3, h + 1):
                        for t in range(TH):
                            chain[0] += 1
                            act_e.activation(work2[:, (2 * (hh % 4) + t) * P:(2 * (hh % 4) + t + 1) * P],
                                             ps[:, 2 * t + hh // 4, (hh % 4) * P:(hh % 4 + 1) * P], ACT.Square,
                                             accum_out=small[:, 460 + 8 * (hh // 4) + 4 * t + hh % 4:461 + 8 * (hh // 4) + 4 * t + hh % 4])\
                                 .then_inc(s_a, 1)
                    act_e.wait_ge(s_a, chain[0])
                    act_e.sem_inc(s_osq, 1)
                    root(4 + h // 4, mean_o)
            for b in (0, 2):
                act_e.wait_ge(s_oT, b + 1)
                act_e.copy(hT[:, 2 * b:2 * b + 2, :], ps[:, 4 + b, :].rearrange("p (h s) -> p h s", h=2))\
                     .then_inc(s_oTc[1], 1)
            act_e.wait_ge(s_x2, 3)
            squares(3)
            copy_hT(8)
            route(1)
            experts(1)
            act_e.wait_ge(s_x2, 4)
            squares(4)

        @block.vector
        def _(ve):
            chain = [0]

            def then(ins):
                chain[0] += 1
                ins.then_inc(s_v, 1)
                ve.wait_ge(s_v, chain[0])

            def norm(count, buf, uses, permuted):
                ve.wait_ge(s_ssq, count + 1)
                ve.wait_ge(gain_in[buf], 16 * uses)
                rstd(count + (1 if count < 3 else 3), ssq, mean_x, rstd_x, D, RMS_EPS)
                for t in range(TH):
                    if permuted:
                        o = h_sb[:, t, :].rearrange("p (k q) -> p q k", k=KT)
                        a = x_sb[:, t, :].rearrange("p (q k) -> p q k", k=KT)
                        g = gain[:, buf, :].rearrange("p (q k) -> p q k", k=KT)
                    else:
                        o, a, g = h_sb[:, t, :], x_sb[:, t, :], gain[:, buf, :]
                    ins = ve.scalar_tensor_tensor(o, a, rstd_x[:, t:t + 1], g, ALU.mult, ALU.mult)
                    then(ins)
                ve.sem_inc(s_h, 1)

            def rstd(number, sums, mean, result, width, eps):
                ve.tensor_scalar(mean, sums, 1.0 / width, eps, ALU.mult, ALU.add).then_inc(s_mean, 1)
                ve.wait_ge(s_root, number)
                then(ve.reciprocal(result, mean))

            def copy_hT(first):
                for b in (1, 3):
                    ve.wait_ge(s_tr, first + b + 1)
                    ve.tensor_copy(hT[:, 2 * b:2 * b + 2, :], ps[:, b, :].rearrange("p (k s) -> p k s", k=2))\
                      .then_inc(s_hT, 1)

            def sm(at, *shape):
                n = int(np.prod(shape))
                v = small[:, at:at + n]
                return v if len(shape) == 1 else v.rearrange("p (a b) -> p a b", a=shape[0])

            def wide(v, n):
                return v.unsqueeze(2).to_broadcast([P, v.shape[1], n])

            def numbers(n):
                return iota[:, 0:n].unsqueeze(1).to_broadcast([P, TH, n])

            def first_max(vals, n, top, hit, index, one):
                then(ve.tensor_reduce(top, vals, AX, ALU.max))
                then(ve.tensor_tensor(hit, vals, wide(top, n), ALU.is_ge))
                then(ve.scalar_tensor_tensor(hit, hit, -BIG, numbers(n), ALU.mult, ALU.add))
                then(ve.tensor_reduce(index, hit, AX, ALU.min))
                then(ve.tensor_scalar(index, index, BIG, None, ALU.add))
                then(ve.tensor_tensor(one, numbers(n), wide(index, n), ALU.is_equal))

            def route(layer):
                L = sm(192, TH, NR)
                hit = sm(264, TH, NE)
                M = sm(328, TH, NE)
                gtop, gidx, gone = sm(392, TH), sm(394, TH), sm(424, TH, NG)
                eg, dg = sm(400, TH, NG), sm(408, TH, NG)
                e2, d2 = sm(416, TH), sm(418, TH)
                v1, v2, idx, gs, gp = sm(480, TH), sm(482, TH), sm(484, TH), sm(486, TH), sm(488, TH)
                den, w1, w2 = sm(490, TH), sm(492, TH), sm(494, TH)
                one1, one2 = sm(512, TH, NE), sm(576, TH, NE)
                ve.wait_ge(s_lg, layer + 1)
                if layer == 0:
                    ve.wait_ge(s_wr, 128)
                then(ve.tensor_tensor(L, ps[:, 5, 0:128].rearrange("p (t n) -> p t n", t=TH)[:, :, 0:NR],
                                      rb[:, layer, :].unsqueeze(1).to_broadcast([P, TH, NR]), ALU.add))
                first_max(L[:, :, 0:NG], NG, gtop, hit[:, :, 0:NG], gidx, gone)
                then(ve.tensor_tensor(dg, L[:, :, 0:NG], wide(gtop, NG), ALU.subtract))
                ve.sem_inc(s_dg, 1)
                then(ve.tensor_scalar(gone, gone, -1.0, PEN, ALU.add, ALU.mult))
                for t in range(TH):
                    then(ve.tensor_tensor(M[:, t, :].rearrange("p (g e) -> p g e", g=NG),
                                          L[:, t, NG:NR].rearrange("p (g e) -> p g e", g=NG),
                                          wide(gone[:, t, :], EPG), ALU.add))
                first_max(M, NE, v1, hit, idx, one1)
                then(ve.scalar_tensor_tensor(M, one1, -3 * PEN, M, ALU.mult, ALU.add))
                first_max(M, NE, v2, hit, idx, one2)
                then(ve.tensor_tensor(d2, v2, v1, ALU.subtract))
                ve.sem_inc(s_dg, 1)
                then(ve.tensor_tensor(A[:, :, :], one1, one2, ALU.add))
                ve.sem_inc(s_A, 1)
                ve.wait_ge(s_eg, 2 * layer + 1)
                then(ve.tensor_reduce(gs, eg, AX, ALU.add))
                ve.wait_ge(s_eg, 2 * layer + 2)
                then(ve.tensor_scalar(den, e2, 1.0, None, ALU.add))
                then(ve.tensor_tensor(den, den, gs, ALU.mult))
                then(ve.reciprocal(w1, den))
                then(ve.tensor_tensor(w2, w1, e2, ALU.mult))
                then(ve.tensor_tensor(one1, one1, wide(w1, NE), ALU.mult))
                then(ve.tensor_tensor(one2, one2, wide(w2, NE), ALU.mult))
                then(ve.tensor_tensor(W[:, :, :], one1, one2, ALU.add))
                ve.wait_ge(s_rk, layer + 1)
                then(ve.scalar_tensor_tensor(R[:, :, :], ps[:, 6, 0:2 * NE].rearrange("p (t e) -> p t e", t=TH), 1.0,
                                             A[:, :, :], ALU.add, ALU.mult))
                then(ve.tensor_scalar(R[:, :, :], R[:, :, :], -1.0, None, ALU.add))
                most = sm(640, NGRP)
                then(ve.tensor_reduce(most, ps[:, 6, 2 * NE:3 * NE].rearrange("p (g e) -> p g e", g=NGRP), AX, ALU.max))
                then(ve.tensor_reduce(sm(640 + NGRP, 1), most, AX, ALU.max))
                then(ve.tensor_copy(cnt[:, :], sm(640, NGRP + 1)))
                if layer == 0:
                    then(ve.memset(ps[:, 5:8, :], 0.0))
                ve.sem_inc(s_route, 1)

            def group(s, g, gl):
                for t in range(TH):
                    ins = ve.tensor_tensor(onehot[:, t, :, :, :],
                                           iota.rearrange("p (b s) -> p b s", b=NB).unsqueeze(2).to_broadcast([P, NB, E4, SB]),
                                           R[:, t, bass.ds(gl * E4, E4)].unsqueeze(1).unsqueeze(3).to_broadcast([P, NB, E4, SB]),
                                           ALU.is_equal)
                ins.then_inc(s["onehot"], 1)
                ve.wait_ge(s["onehot"], g + 1)
                for t in range(TH):
                    ins = ve.tensor_tensor(gated[:, t, :, :, :], onehot[:, t, :, :, :],
                                           W[:, t, bass.ds(gl * E4, E4)].unsqueeze(1).unsqueeze(3).to_broadcast([P, NB, E4, SB]),
                                           ALU.mult)
                ins.then_inc(s["gated"], 1)
                for k in range(E4):
                    n1 = g * E4 + (k + 1)
                    ve.wait_ge(s["exp"], n1)
                    ve.tensor_scalar(sg[:, 1, :, :], sg[:, 0, :, :], 1.0, None, ALU.add).then_inc(s["den"], 1)
                    ve.wait_ge(s["den"], n1)
                    ve.reciprocal(sg[:, 2, :, :], sg[:, 1, :, :]).then_inc(s["sig"], 1)
                    ve.wait_ge(s["sig"], n1)
                    ve.tensor_tensor(sg[:, 3, :, :], sg[:, 2, :, :], gu_ps[:, :, 0, :], ALU.mult).then_inc(s["gh"], 1)
                    ve.wait_ge(s["gh"], n1)
                    ve.tensor_tensor(act[:, :, :], sg[:, 3, :, :], gu_ps[:, :, 1, :], ALU.mult).then_inc(s["act"], 1)
                    ve.wait_ge(s["at"], n1)
                    ve.tensor_copy(actT[:, :, :], at_ps).then_inc(s["atc"], 1)
                ve.wait_ge(s["gt"], g + 1)
                ve.tensor_copy(gateT[:, :, :], gt_ps).then_inc(s["gtc"], 1)

            def experts(layer):
                with ve.Fori(0, NGRP) as g:
                    group(main, g + layer * NGRP, g)
                fb = more[layer]
                most = ve.value_load(cnt[0:1, NGRP:NGRP + 1], min_val=0, max_val=S)
                with ve.If(most > CAP):
                    with ve.Fori(0, PASSES - 1) as m:
                        with ve.If(most > CAP * m + CAP):
                            ve.tensor_scalar(R[:, :, :], R[:, :, :], -float(CAP), None, ALU.add).then_inc(fb["shift"], 1)
                            with ve.Fori(0, NGRP) as g:
                                ve.wait_ge(fb["shift"], m + 1)
                                group(fb, m * NGRP + g, g)
                                ve.wait_ge(fb["sc"], m * NGRP + g + 1)
                ve.wait_ge(main["sc"], NGRP * (layer + 1))
                residual()

            def residual():
                for t in range(TH):
                    for i in range(2):
                        xs = x_sb[:, t, 512 * i:512 * (i + 1)]
                        ins = ve.tensor_tensor(xs, xs, ps[:, 2 * t + i, :], ALU.add)
                        then(ins)
                ve.sem_inc(s_x2, 1)

            ve.memset(zero, 0.0).then_inc(s_z, 1)
            ve.wait_ge(s_x, 16)
            norm(0, 0, 1, False)
            for g in (0, 2):
                ve.wait_ge(s_mix, g + 1)
                ve.tensor_copy(mixT[:, 2 * g:2 * g + 2, :], ps[:, g, :].rearrange("p (m s) -> p m s", m=2))\
                  .then_inc(s_mixT[0], 1)
            ve.wait_ge(s_po, 1)
            ve.wait_ge(gain_in[1], 16)
            for t in range(TH):
                then(ve.tensor_tensor(h_sb[:, t, :], gain[:, 1, :], ps[:, 4 + 2 * t:6 + 2 * t, :].rearrange("p a b -> p (a b)"),
                                      ALU.mult))
                then(ve.tensor_tensor(x_sb[:, t, :], x_sb[:, t, :], h_sb[:, t, :], ALU.add))
            ve.sem_inc(s_x2, 1)
            norm(1, 0, 2, True)
            copy_hT(0)
            ve.wait_ge(s_c, 16)
            route(0)
            experts(0)

            ve.wait_ge(s_lam, 80)
            for i in range(2):
                then(ve.tensor_tensor(small[:, 700:764], lam4[:, 2 * i, :], lam4[:, 2 * i + 1, :], ALU.mult))
                then(ve.tensor_reduce(small[:, 432 + i:433 + i], small[:, 700:764], AX, ALU.add))
            ve.sem_inc(s_ls, 1)
            norm(2, 1, 2, True)
            ve.wait_ge(s_le, 1)
            lam = small[:, 436:437]
            then(ve.tensor_tensor(lam, small[:, 434:435], small[:, 435:436], ALU.subtract))
            then(ve.tensor_scalar(lam, lam, LAM_INIT, None, ALU.add))
            then(ve.tensor_scalar(subg[:, :], subg[:, :], 1.0 - LAM_INIT, None, ALU.mult))
            copy_hT(4)
            ve.wait_ge(s_q, 1)
            for b in (1, 3):
                ve.tensor_scalar(qT[:, 2 * b:2 * b + 2, :], ps[:, b, :].rearrange("p (h s) -> p h s", h=2), HD ** -0.5,
                                 None, ALU.mult).then_inc(s_qc, 1)
            ve.wait_ge(s_q, 2)
            for b in (1, 3):
                ve.tensor_copy(kT[:, 2 * b:2 * b + 2, :], ps[:, 4 + b, :].rearrange("p (h s) -> p h s", h=2))\
                  .then_inc(s_kc, 1)

            def logits(h):
                ve.wait_ge(s_S, h + 1)
                if h >= 2:
                    ve.wait_ge(s_ex, 4 * (h - 1))
                for c in range(2):
                    ve.scalar_tensor_tensor(prob[:, h % 2, c, :], dist, -(2.0 ** (-8.0 * (h + 1) / NH)),
                                            ps[:, 4 + 2 * (h % 2) + c, 0:LW], ALU.mult, ALU.add).then_inc(s_L, 1)
                ve.wait_ge(s_L, 2 * (h + 1))
                for c in range(2):
                    for t, cols in ((0, slice(0, P)), (1, slice(P, LW))):
                        at = 440 + 8 * (h % 2) + 2 * c + t
                        ve.tensor_reduce(small[:, at:at + 1], prob[:, h % 2, c, cols], AX, ALU.max, negate=True)\
                          .then_inc(s_m, 1)

            def weights(h):
                ve.wait_ge(s_ex, 4 * (h + 1))
                at = 444 + 8 * (h % 2)
                r = small[:, 770:774]
                then(ve.reciprocal(r, small[:, at:at + 4]))
                then(ve.tensor_scalar(r[:, 2:4], r[:, 2:4], lam, None, ALU.mult))
                for t, cols in ((0, slice(0, P)), (1, slice(P, LW))):
                    ins = ve.tensor_scalar(prob[:, h % 2, 1, cols], prob[:, h % 2, 1, cols], r[:, 2 + t:3 + t], None, ALU.mult)
                then(ins)
                ve.scalar_tensor_tensor(kT[:, h, 0:P], prob[:, h % 2, 0, 0:P], r[:, 0:1], prob[:, h % 2, 1, 0:P],
                                        ALU.mult, ALU.subtract)
                then(ve.scalar_tensor_tensor(qT[:, h, :], prob[:, h % 2, 0, P:LW], r[:, 1:2], prob[:, h % 2, 1, P:LW],
                                             ALU.mult, ALU.subtract))
                ve.sem_inc(s_p, 1)

            for h in range(NH + 1):
                if h < NH:
                    logits(h)
                if h >= 1:
                    weights(h - 1)
            ve.wait_ge(s_vp, 1)
            for b in (1, 3):
                ve.tensor_copy(v_sb[:, b // 2, 512:1024], ps[:, b, :]).then_inc(s_vs, 1)
            for q in range(2):
                ve.wait_ge(s_osq, q + 1)
                sums = small[:, 460 + 8 * q:468 + 8 * q]
                rs = rstd_o
                rstd(4 + q, sums, mean_o, rs, 2 * HD, SUB_EPS)
                for t in range(TH):
                    for hh in range(4):
                        h = 4 * q + hh
                        ins = ve.scalar_tensor_tensor(h_sb[:, t, h * P:(h + 1) * P], ps[:, 2 * t + q, hh * P:(hh + 1) * P],
                                                      rs[:, 4 * t + hh:4 * t + hh + 1], subg[:, :], ALU.mult, ALU.mult)
                ins.then_inc(s_os, 1)
            for b in (1, 3):
                ve.wait_ge(s_oT, b + 1)
                ve.tensor_copy(hT[:, 2 * b:2 * b + 2, :], ps[:, 4 + b, :].rearrange("p (h s) -> p h s", h=2))\
                  .then_inc(s_oTc[0], 1)
            ve.wait_ge(s_wo, 1)
            residual()
            norm(3, 0, 3, True)
            copy_hT(8)
            route(1)
            experts(1)
            norm(4, 1, 3, False)


_INS = ["x", "norm_mix_g", "norm_ffn_g", "pool_w", "pool_scale", "attn_wq", "attn_wk", "attn_wv", "attn_wo",
        "attn_lq1", "attn_lk1", "attn_lq2", "attn_lk2", "attn_subln_g", "moe_wg", "moe_bg", "moe_we", "moe_be",
        "moe_w1", "moe_w3", "moe_w2", "final_g"]


def kernel(**inputs):
    import concourse.bacc as bacc
    from concourse.bass_utils import run_bass_kernel_spmd

    nc = bacc.Bacc("TRN2", target_bir_lowering=False, num_devices=1)
    arrays, args = {}, []
    for name in _INS + ["consts"]:
        a = shape_constants() if name == "consts" else np.ascontiguousarray(inputs[name])
        arrays[f"in_{name}"] = a
        args.append(nc.dram_tensor(f"in_{name}", a.shape, mybir.dt.from_np(a.dtype), kind="ExternalInput").ap())
    args.append(nc.dram_tensor("out_x", (1, S, D), F32, kind="ExternalOutput").ap())
    build(nc, *args)
    r = run_bass_kernel_spmd(nc, [arrays], core_ids=[0])
    return r.results[0]["out_x"]
```

```python
import math
from contextlib import ExitStack

import numpy as np

import concourse.bass as bass
from concourse import mybir

F32 = mybir.dt.float32
I32 = mybir.dt.int32
ALU = mybir.AluOpType
ACT = mybir.ActivationFunctionType
AX = mybir.AxisListType.X

P = 128
S, D = 256, 1024
TH = S // P
KT = D // P
NH, HD = 8, 64
NG, EPG = 4, 8
NE = NG * EPG
F = 512
JT = F // P
SB = 32
NB = 2
CAP = SB * NB
PASSES = S // CAP
E4 = P // SB
GPB = 2
BODY = GPB * E4
ITERS = NE // BODY
NGRP = NE // E4
RING = 8
CH = 4096
CPE = 3
ACH = 8
WINDOWS = (2, 4, 8, 16)
RMS_EPS, SUB_EPS = 1e-6, 1e-5
BIG = 1024.0
PEN = 1e30
LAM_INIT = 0.8 - 0.6 * math.exp(-0.3)
LW = P + S
NR = NG + NE
assert (CPE * NE) % RING == 0 and ACH % RING == 0 and (CPE * BODY) % RING == 0

C_ID, C_U, C_ONE, C_DIST = 0, P, 2 * P, 3 * P
C_IOTA = C_DIST + LW
C_BAND = C_IOTA + CAP
BW = S + P
C_ALL = C_BAND + len(WINDOWS) * BW


WARM = (2, 2, 3, 5, 3)


def shape_constants():
    c = np.zeros((P, C_ALL), np.float32)
    i = np.arange(P)
    c[:, C_ID:C_ID + P] = np.eye(P)
    c[:, C_U:C_U + P] = i[:, None] < i[None, :]
    c[:, C_ONE:C_ONE + P] = 1.0
    for half, at, keys in ((0, 0, P), (1, P, S)):
        q, k = i[:, None] + half * P, np.arange(keys)[None, :]
        c[:, C_DIST + at:C_DIST + at + keys] = np.where(k // 64 <= q // 64, np.abs(q - k), 1e33)
    c[:, C_IOTA:C_IOTA + CAP] = np.arange(CAP)
    for g, win in enumerate(WINDOWS):
        t = np.arange(S)
        lag = t[None, :] - t[:, None]
        band = ((lag >= 0) & (lag < win)) / np.minimum(t + 1, win)[None, :] - (lag == 0)
        at = C_BAND + g * BW
        c[:, at:at + S] = band[:P]
        c[:, at + S:at + BW] = band[P:, P:]
    return c


def build(nc, x, norm_mix_g, norm_ffn_g, pool_w, pool_scale, wq, wk, wv, wo, lq1, lk1, lq2, lk2, subln_g,
          moe_wg, moe_bg, moe_we, moe_be, moe_w1, moe_w3, moe_w2, final_g, consts, out):
    with ExitStack() as ctx:
        def sb(name, shape, dt=F32):
            return ctx.enter_context(nc.sbuf_tensor(name, shape, dt))

        def sem(name):
            return ctx.enter_context(nc.semaphore(name))

        ring = sb("ring", [P, RING, CH])
        x_sb = sb("x_sb", [P, TH, D])
        h_sb = sb("h_sb", [P, TH, D])
        hT = sb("hT", [P, KT, S])
        gain = sb("gain", [P, 2, D])
        cst = sb("cst", [P, C_BAND])
        work = sb("work", [P, 6144])
        work2 = sb("work2", [P, 2304])
        wr = sb("wr", [P, 2, KT, NR])
        rb = sb("rb", [P, 2, NR])
        lam4 = sb("lam4", [P, 4, HD])
        subg = sb("subg", [P, 2 * HD])
        R = sb("R", [P, TH, NE + E4])
        W = sb("W", [P, TH, NE])
        A = sb("A", [P, TH, NE])
        small = sb("small", [P, 1088])
        cnt = sb("cnt", [P, NE + NGRP + 1], I32)
        ident, upper, ones = (cst[:, c:c + P] for c in (C_ID, C_U, C_ONE))
        dist = cst[:, C_DIST:C_DIST + LW]
        iota = cst[:, C_IOTA:C_IOTA + CAP]

        zero = small[:, 64:64 + P]
        mean_o, newt_o = small[:, 466:468], small[:, 468:470]
        eps_x, eps_o = small[:, 8:9], small[:, 9:10]
        ssq, mean_x, root_x, newt_x = (small[:, c:c + 2] for c in (0, 2, 4, 6))
        junk_o = small[:, 800:1056].rearrange("p (t e) -> p t e", t=TH)
        ffn0 = work2[:, 1024:1024 + D]
        we_raw = work[:, 5632:6144].rearrange("p (l n) -> p l n", l=2)
        wg_raw = work2[:, 0:64].rearrange("p (l n) -> p l n", l=2)

        band = work[:, 0:len(WINDOWS) * BW]
        pw = work[:, 1536:1536 + 2048].rearrange("p (g c d) -> p g c d", g=4, c=2)
        mixT = work[:, 3584:3584 + 2048].rearrange("p (m s) -> p m s", m=KT)
        qT = work[:, 0:2048].rearrange("p (h s) -> p h s", h=NH)
        kT = work[:, 2048:4096].rearrange("p (h s) -> p h s", h=NH)
        v_sb = work[:, 4096:6144].rearrange("p (t n) -> p t n", t=TH)
        prob = work2[:, 0:4 * LW].rearrange("p (b c w) -> p b c w", b=2, c=2)
        aT = work2[:, 4 * LW:6 * LW].rearrange("p (b w) -> p b w", b=2)
        xg = work[:, 0:512].rearrange("p (k c) -> p k c", k=KT)
        sg = work[:, 512:1536].rearrange("p (m b f) -> p m b f", m=4, b=NB)
        act = work[:, 1536:1792].rearrange("p (b f) -> p b f", b=NB)
        actT = work[:, 1792:2048].rearrange("p (b r) -> p b r", b=NB)
        y = work[:, 2048:4096].rearrange("p (b n) -> p b n", b=NB)
        onehot = work2[:, 0:512].rearrange("p (t b e s) -> p t b e s", t=TH, b=NB, e=E4)
        gated = work2[:, 512:1024].rearrange("p (t b e s) -> p t b e s", t=TH, b=NB, e=E4)
        gateT = work2[:, 1024:1536].rearrange("p (b s) -> p b s", b=NB)

        ps = ctx.enter_context(nc.psum_tensor("ps", [P, 8, 512], F32))
        acc = ps[:, 0:4, :].rearrange("p (t n) w -> p t n w", t=TH)
        xg_ps = ps[:, 4, :].rearrange("p (k c) -> p k c", k=KT)
        gu_ps = ps[:, 5, :].rearrange("p (b m f) -> p b m f", b=NB, m=2)
        gt_ps = ps[:, 5, :].rearrange("p (b s) -> p b s", b=NB)
        y_ps = ps[:, 6, :].rearrange("p (b n) -> p b n", b=NB)
        at_ps = ps[:, 7, 0:256].rearrange("p (b r) -> p b r", b=NB)

        loaded = [sem(f"loaded{i}") for i in range(RING)]
        s_w = sem("s_w")
        s_x = [sem("s_x0"), sem("s_x1")]
        s_c, s_band, s_pw, s_wraw, s_rb, s_lam = (sem(n) for n in ("s_c", "s_band", "s_pw", "s_wraw", "s_rb", "s_lam"))
        s_mix0, s_scale, s_ffn0 = sem("s_mix0"), sem("s_scale"), sem("s_ffn0")
        s_wr = sem("s_wr")
        gain_in = [sem("gain_in0"), sem("gain_in1")]
        s_out = sem("s_out")
        s_ssq = sem("s_ssq")
        s_root = sem("s_root")
        s_x2 = sem("s_x2")
        s_h = sem("s_h")
        s_mix, s_po = sem("s_mix"), sem("s_po")
        s_mixT = [sem("s_mixT_v"), sem("s_mixT_a")]
        s_tr = sem("s_tr")
        s_hT = [sem("s_hT_v"), sem("s_hT_a")]
        s_lg, s_A, s_rk, s_route = sem("s_lg"), sem("s_A"), sem("s_rk"), sem("s_route")
        s_dg, s_eg = sem("s_dg"), sem("s_eg")
        s_v = sem("s_v")
        s_a = sem("s_a")
        s_z = sem("s_z")
        s_vp = sem("s_vp")
        s_vs = [sem("s_vs_v"), sem("s_vs_a")]
        s_q, s_qc = sem("s_q"), sem("s_qc")
        s_k = sem("s_k")
        s_S, s_L, s_ex, s_p = sem("s_S"), sem("s_L"), sem("s_ex"), sem("s_p")
        s_m = sem("s_m")
        s_aT, s_aTc, s_o = sem("s_aT"), sem("s_aTc"), sem("s_o")
        s_osq, s_oroot, s_os = sem("s_osq"), sem("s_oroot"), sem("s_os")
        s_oT, s_oTc, s_wo = sem("s_oT"), sem("s_oTc"), sem("s_wo")
        s_ls, s_le = sem("s_ls"), sem("s_le")

        STEPS = ("onehot", "gated", "xg", "xgc", "half", "gu", "exp", "den", "sig", "gh", "act", "at", "atc", "y", "yc",
                 "gt", "gtc", "sc", "shift", "passed", "wl0", "wl1", "wl2")

        def moe_sems(name):
            return {k: sem(f"{name}_{k}") for k in STEPS}

        main = moe_sems("m")
        more = [moe_sems("p0"), moe_sems("p1")]

        def use_before(layer):
            return layer * (CPE * NE + ACH) // RING

        def chunk_parts(layer, e, j):
            if j < 2:
                return [(m * 2048, w[layer, e, :, :].rearrange("(p k) n -> p k n", k=KT)[:, 4 * j:4 * j + 4, :])
                        for m, w in ((0, moe_w1), (1, moe_w3))]
            w = moe_w2[layer, e, :, :].rearrange("(j p) n -> p j n", p=P)
            return [(m * 2048, w[:, 2 * m:2 * m + 2, :]) for m in range(2)]

        def attn_parts(c):
            w = (wv, wq, wk, wo)[c // 2]
            if c < 6:
                w = w[0].rearrange("(p k) n -> p k n", k=KT)
            else:
                w = w[0].rearrange("(k p) n -> p k n", p=P)
            at = 4 * (c % 2)
            return [(m * 2048, w[:, at + 2 * m:at + 2 * m + 2, :]) for m in range(2)]

        def view(src):
            return src.shape[1], src.shape[2]

        block = ctx.enter_context(nc.Block())

        @block.sync
        def _(sp):
            def load(slot, parts, signal):
                for at, src in parts:
                    k, n = view(src)
                    sp.dma_start(ring[:, slot, at:at + k * n].rearrange("p (k n) -> p k n", k=k), src) \
                      .then_inc(signal, 16)

            def row(dst, src):
                return sp.dma_start(dst, src.to_broadcast([P] + list(src.shape[1:])))

            for t in range(TH):
                sp.dma_start(x_sb[:, t, :], x[0, t * P:(t + 1) * P, :]).then_inc(s_x[t], 16)
            row(gain[:, 0, :], norm_mix_g[0:1, :]).then_inc(s_mix0, 16)
            sp.dma_start(band, consts[:, C_BAND:C_ALL]).then_inc(s_band, 16)
            sp.dma_start(pw, pool_w[0].rearrange("g (c p) d -> p g c d", p=P)).then_inc(s_pw, 16)
            row(gain[:, 1, :], pool_scale[0:1, :]).then_inc(s_scale, 16)
            row(ffn0, norm_ffn_g[0:1, :]).then_inc(s_ffn0, 16)
            sp.dma_start(cst[:, :], consts[:, 0:C_BAND]).then_inc(s_c, 16)
            sp.dma_start(wg_raw, moe_wg.rearrange("l (p k) n -> p l (k n)", k=KT)).then_inc(s_wraw, 16)
            sp.dma_start(we_raw, moe_we.rearrange("l (p k) n -> p l (k n)", k=KT)).then_inc(s_wraw, 16)
            for layer in range(2):
                row(rb[:, layer, 0:NG], moe_bg[layer:layer + 1, :]).then_inc(s_rb, 16)
                row(rb[:, layer, NG:NR], moe_be[layer:layer + 1, :]).then_inc(s_rb, 16)
            used = (main["half"], main["gu"], main["y"])
            attn_used = ((s_vp, 2), (s_vp, 2), (s_q, NH), (s_q, NH), (s_q, NH), (s_q, NH), (s_wo, 2), (s_wo, 2))
            for layer in range(2):
                for c in range(RING):
                    if layer == 1:
                        sp.wait_ge(*attn_used[c])
                    load(c, chunk_parts(layer, c // CPE, c % CPE), loaded[c])
                steady = CPE * BODY

                def stream(it, c):
                    e, j = divmod(c - RING, CPE)
                    sp.wait_ge(used[j], it * BODY + (layer * NE + e + 1))
                    load(c % RING, chunk_parts(layer, it * BODY + c // CPE, c % CPE), loaded[c % RING])

                with sp.Fori(0, ITERS - 1) as it:
                    for c in range(RING, RING + steady):
                        stream(it, c)
                for c in range(RING, steady):
                    stream(ITERS - 1, c)
                fb = more[layer]
                sp.wait_ge(s_route, layer + 1)
                most = sp.value_load(cnt[0:1, NE + NGRP:NE + NGRP + 1], min_val=0, max_val=S)
                with sp.If(most > CAP):
                    sp.wait_ge(main["y"], NE * (layer + 1))
                    with sp.Fori(0, PASSES - 1) as m:
                        with sp.If(most > CAP * m + CAP):
                            with sp.Fori(0, NE) as e:
                                n = m * NE + e
                                for j in range(CPE):
                                    load(j, chunk_parts(layer, e, j), fb[f"wl{j}"])
                                sp.wait_ge(fb["y"], n + 1)
                                sp.sem_inc(fb["passed"], 1)
                if layer == 0:
                    for c in range(ACH):
                        e, j = divmod(CPE * NE - RING + c, CPE)
                        sp.wait_ge(used[j], e + 1)
                        load(c, attn_parts(c), loaded[c])
            for t in range(TH):
                sp.wait_ge(s_h, 2 * 4 + t + 1)
                sp.dma_start(out[0, t * P:(t + 1) * P, :], h_sb[:, t, :]).then_inc(s_out, 16)
            sp.wait_ge(s_out, 32)

        @block.gpsimd
        def _(pool):
            def row(dst, src):
                return pool.dma_start(dst, src.to_broadcast([P] + list(src.shape[1:])))

            for i, w in enumerate((lq1, lk1, lq2, lk2)):
                row(lam4[:, i, :], w[0:1, :]).then_inc(s_lam, 16)
            row(subg[:, :], subln_g[0:1, :]).then_inc(s_lam, 16)
            pool.wait_ge(s_wraw, 32)
            for layer in range(2):
                pool.tensor_copy(wr[:, layer, :, 0:NG], wg_raw[:, layer, :].rearrange("p (k n) -> p k n", k=KT)).then_inc(s_wr, 1)
                pool.tensor_copy(wr[:, layer, :, NG:NR], we_raw[:, layer, :].rearrange("p (k n) -> p k n", k=KT)).then_inc(s_wr, 1)
            pool.wait_ge(s_h, 2)
            row(gain[:, 0, :], norm_mix_g[1:2, :]).then_inc(gain_in[0], 16)
            pool.wait_ge(s_x2, 2)
            row(gain[:, 1, :], norm_ffn_g[1:2, :]).then_inc(gain_in[1], 16)
            pool.wait_ge(s_h, 6)
            row(gain[:, 0, :], final_g.rearrange("(a d) -> a d", a=1)).then_inc(gain_in[0], 16)

        @block.tensor
        def _(pe):
            def transposes(count):
                for t in range(TH):
                    pe.wait_ge(s_h, 2 * count + t + 1)
                    for k in range(KT):
                        mm = pe.transpose(ps[:, 2 * t + k // 4, (k % 4) * P:(k % 4 + 1) * P],
                                          h_sb[:, t, k * P:(k + 1) * P], ident)
                        if k % 4 == 3:
                            mm.then_inc(s_tr, 1)

            def keep_clock(products, bank):
                for _ in range(products):
                    pe.matmul(ps[:, bank, :], zero, cst[:, 0:512], start=True, stop=True)

            def wait_hT(number, t):
                for s in s_hT:
                    pe.wait_ge(s, 2 * number + t + 1)

            def route(layer, number):
                if layer == 0:
                    pe.wait_ge(s_wr, 4)
                for t in range(TH):
                    wait_hT(number, t)
                    for k in range(KT):
                        mm = pe.matmul(ps[:, 5, t * 64:t * 64 + NR], hT[:, k, t * P:(t + 1) * P],
                                       wr[:, layer, k, :], start=(k == 0), stop=(k == KT - 1))
                mm.then_inc(s_lg, 1)
                for b in range(4):
                    pe.matmul(ps[:, b, :], zero, cst[:, 0:512], start=True, stop=True)
                keep_clock(WARM[0], 0)
                pe.wait_ge(s_A, layer + 1)
                pe.matmul(ps[:, 6, 0:NE], upper, A[:, 0, :], start=True, stop=True)
                pe.matmul(ps[:, 6, NE:2 * NE], ones, A[:, 0, :], start=True, stop=False)
                pe.matmul(ps[:, 6, NE:2 * NE], upper, A[:, 1, :], start=False, stop=True)
                pe.matmul(ps[:, 6, 2 * NE:3 * NE], ones, A[:, 0, :], start=True, stop=False)
                pe.matmul(ps[:, 6, 2 * NE:3 * NE], ones, A[:, 1, :], start=False, stop=True).then_inc(s_rk, 1)
                keep_clock(WARM[1], 0)

            def group(s, g, placed, fullest, tokens, chunk):
                def by_count(count, step):
                    if count is None:
                        step(NB)
                    else:
                        with pe.If(count > SB):
                            step(NB)
                        with pe.Else():
                            step(1)

                def gather(k):
                    for kt in range(KT):
                        for t in range(TH):
                            mm = pe.matmul(xg_ps[:, kt, :], h_sb[:, t, kt * P:(kt + 1) * P],
                                           onehot[:, t, :, k, :], start=(t == 0), stop=(t == TH - 1))
                    mm.then_inc(s["xg"], 1)

                def expert(k, blocks):
                    n1 = g * E4 + k + 1
                    for half in range(2):
                        w = ring[:, chunk(k, half), :].rearrange("p (m k n) -> p m k n", m=2, k=4)
                        for b in reversed(range(blocks)):
                            for q in range(4):
                                for j in range(JT):
                                    mm = pe.matmul(gu_ps[SB * j:SB * (j + 1), b, :, :],
                                                   xg[:, 4 * half + q, SB * b:SB * (b + 1)],
                                                   w[:, :, q, P * j:P * (j + 1)],
                                                   start=(half == 0 and q == 0 and b == blocks - 1),
                                                   stop=(half == 1 and q == 3), skip_group_check=True)
                        mm.then_inc(s["half"] if half == 0 else s["gu"], 1)
                    if k + 1 < E4:
                        gather(k + 1)
                    pe.wait_ge(s["act"], n1)
                    for b in range(blocks):
                        mm = pe.transpose(at_ps[:, b, :], act[:, b, :], ident)
                    mm.then_inc(s["at"], 1)
                    if k == E4 - 1:
                        pe.wait_ge(s["gated"], g + 1)
                        for b in range(NB):
                            for t in range(TH):
                                mm = pe.transpose(gt_ps[:, b, t * P:(t + 1) * P],
                                                  gated[:, t, b, :, :].rearrange("p e s -> p (e s)"), ident)
                        mm.then_inc(s["gt"], 1)
                    pe.wait_ge(s["atc"], n1)
                    if k > 0:
                        pe.wait_ge(s["yc"], n1 - 1)
                    w = ring[:, chunk(k, 2), :].rearrange("p (j n) -> p j n", j=JT)
                    for b in range(blocks):
                        for j in range(JT):
                            for i in range(4):
                                mm = pe.matmul(y_ps[SB * i:SB * (i + 1), b, :], actT[:, b, SB * j:SB * (j + 1)],
                                               w[:, j, 256 * i:256 * (i + 1)], start=(j == 0), stop=(j == JT - 1))
                    mm.then_inc(s["y"], 1)

                def scatter(blocks):
                    for b in range(blocks):
                        for t in range(TH):
                            for i in range(2):
                                mm = pe.matmul(acc[:, t, i, :], gateT[:, b, t * P:(t + 1) * P],
                                               y[:, b, 512 * i:512 * (i + 1)], start=False, stop=False,
                                               skip_group_check=True)
                    mm.then_inc(s["sc"], 1)

                pe.wait_ge(s["onehot"], placed)
                gather(0)
                for k in range(E4):
                    pe.wait_ge(s["xgc"], g * E4 + k + 1)
                    by_count(tokens(k), lambda blocks, k=k: expert(k, blocks))
                pe.wait_ge(s["gtc"], g + 1)
                pe.wait_ge(s["yc"], g * E4 + E4)
                by_count(fullest, scatter)

            def experts(layer):
                u0 = use_before(layer)
                pe.wait_ge(s_route, layer + 1)
                with pe.Fori(0, ITERS) as it:
                    for gg in range(GPB):
                        g = it * GPB + (layer * NGRP + gg)
                        fullest = pe.value_load(cnt[0:1, bass.ds(it * GPB + (NE + gg), 1)], min_val=0, max_val=S)

                        def tokens(k, gg=gg):
                            return pe.value_load(cnt[0:1, bass.ds(it * BODY + (gg * E4 + k), 1)], min_val=0, max_val=S)

                        def chunk(k, j, gg=gg):
                            c = CPE * (gg * E4 + k) + j
                            pe.wait_ge(loaded[c % RING], (it * (CPE * BODY // RING) + (u0 + c // RING + 1)) * 32)
                            return c % RING

                        group(main, g, it * GPB + (layer * (NGRP + 1) + gg + 1), fullest, tokens, chunk)
                fb = more[layer]
                most = pe.value_load(cnt[0:1, NE + NGRP:NE + NGRP + 1], min_val=0, max_val=S)
                with pe.If(most > CAP):
                    with pe.Fori(0, PASSES - 1) as m:
                        with pe.If(most > CAP * m + CAP):
                            with pe.Fori(0, NGRP) as gg:
                                g = m * NGRP + gg

                                def chunk(k, j):
                                    pe.wait_ge(fb[f"wl{j}"], (g * E4 + (k + 1)) * 32)
                                    return j

                                group(fb, g, m * (NGRP + 1) + gg + 1, None, lambda k: None, chunk)

            pe.wait_ge(s_h, 2)
            pe.wait_ge(s_band, 16)
            for m in range(KT):
                at = (m // 2) * BW
                o = ps[:, m // 2, (m % 2) * S:(m % 2 + 1) * S]
                pe.matmul(o, h_sb[:, 0, m * P:(m + 1) * P], band[:, at:at + S], start=True, stop=False)
                mm = pe.matmul(o[:, P:S], h_sb[:, 1, m * P:(m + 1) * P], band[:, at + S:at + BW], start=False, stop=True)
                if m % 2 == 1:
                    mm.then_inc(s_mix, 1)
            pe.wait_ge(s_pw, 16)
            for t in range(TH):
                for g in range(4):
                    if t == 0:
                        pe.wait_ge(s_mixT[g % 2], g // 2 + 1)
                    for c in range(2):
                        mm = pe.matmul(ps[:, 4 + 2 * t + g // 2, (g % 2) * S:(g % 2 + 1) * S],
                                       mixT[:, 2 * g + c, t * P:(t + 1) * P], pw[:, g, c, :],
                                       start=(c == 0), stop=(c == 1))
                mm.then_inc(s_po, 1)
            pe.wait_ge(s_z, 1)
            pe.wait_ge(s_c, 16)
            keep_clock(WARM[2], 0)
            transposes(1)
            route(0, 0)
            experts(0)

            keep_clock(WARM[3], 7)
            transposes(2)
            u = CPE * NE // RING + 1

            def matrix(c, kt):
                return ring[:, c + kt // 4, :].rearrange("p (k n) -> p k n", k=4)[:, kt % 4, :]

            for t in range(TH):
                wait_hT(1, t)
                for kt in range(KT):
                    if t == 0 and kt % 4 == 0:
                        pe.wait_ge(loaded[kt // 4], 32 * u)
                    for i in range(2):
                        mm = pe.matmul(ps[:, 2 * t + i, :], hT[:, kt, t * P:(t + 1) * P],
                                       matrix(0, kt)[:, 512 * i:512 * (i + 1)], start=(kt == 0), stop=(kt == KT - 1))
                mm.then_inc(s_vp, 1)

            def queries_keys(h):
                if h < 2:
                    pe.wait_ge(s_vs[1 - h], 1)
                else:
                    pe.wait_ge(s_qc, h - 1)
                for i in range(2):
                    for kt in range(KT):
                        if h == 0 and kt % 4 == 0:
                            pe.wait_ge(loaded[2 + 2 * i + kt // 4], 32 * u)
                        mm = pe.matmul(ps[:, h % 2, i * S:(i + 1) * S], matrix(2 + 2 * i, kt)[:, h * P:(h + 1) * P],
                                       hT[:, kt, :], start=(kt == 0), stop=(kt == KT - 1))
                mm.then_inc(s_q, 1)

            def scores(h):
                pe.wait_ge(s_qc, h + 1)
                if h == 0:
                    for s in s_vs:
                        pe.wait_ge(s, 2)
                else:
                    pe.wait_ge(s_L, 2 * h)
                for queries, keys in ((slice(0, P), slice(0, P)), (slice(P, S), slice(0, S))):
                    for c in range(2):
                        r = slice(HD * c, HD * (c + 1))
                        cols = slice(queries.start, queries.start + keys.stop)
                        mm = pe.matmul(ps[:, 2 + c, cols], qT[r, h, queries], kT[r, h, keys], start=True, stop=True)
                mm.then_inc(s_S, 1)

            def turn_weights(h):
                pe.wait_ge(s_p, h + 1)
                if h >= 2:
                    pe.wait_ge(s_aTc, h - 1)
                bank = ps[:, 4 + 3 * (h % 2), :]
                pe.transpose(bank[:, 0:P], kT[:, h, 0:P], ident)
                pe.transpose(bank[:, P:2 * P], qT[:, h, 0:P], ident)
                pe.transpose(bank[:, 2 * P:3 * P], qT[:, h, P:S], ident).then_inc(s_aT, 1)

            def attend(h):
                pe.wait_ge(s_aTc, h + 1)
                if h >= 2:
                    pe.wait_ge(s_oTc, h - 1)
                bank, e = ps[:, 5 + h % 2, :], slice(h * P, (h + 1) * P)
                pe.matmul(bank[:, 0:P], aT[:, h % 2, 0:P], v_sb[:, 0, e], start=True, stop=True)
                pe.matmul(bank[:, P:S], aT[:, h % 2, P:2 * P], v_sb[:, 0, e], start=True, stop=False)
                pe.matmul(bank[:, P:S], aT[:, h % 2, 2 * P:3 * P], v_sb[:, 1, e], start=False, stop=True)\
                  .then_inc(s_o, 1)

            def turn_output(h):
                pe.wait_ge(s_os, h + 1)
                for t in range(TH):
                    mm = pe.transpose(ps[:, 5 + h % 2, S + t * P:S + (t + 1) * P], h_sb[:, t, h * P:(h + 1) * P], ident)
                mm.then_inc(s_oT, 1)

            def project(t, heads):
                for h in heads:
                    if h % 4 == 0:
                        pe.wait_ge(loaded[6 + h // 4], 32 * u)
                    pe.wait_ge(s_oTc, h + 1)
                    for i in range(2):
                        mm = pe.matmul(ps[:, 2 * t + i, :], qT[:, h, t * P:(t + 1) * P],
                                       matrix(6, h)[:, 512 * i:512 * (i + 1)], start=(h == 0), stop=(h == NH - 1))
                if heads[-1] == NH - 1:
                    mm.then_inc(s_wo, 1)

            for h in range(NH + 4):
                if h < NH:
                    queries_keys(h)
                if 1 <= h <= NH:
                    scores(h - 1)
                if 2 <= h <= NH + 1:
                    turn_weights(h - 2)
                if 3 <= h <= NH + 2:
                    attend(h - 3)
                if 4 <= h:
                    turn_output(h - 4)
                if h == NH:
                    project(0, range(0, 4))
                if h == NH + 1:
                    project(0, range(4, 5))
                    pe.wait_ge(s_L, 2 * NH)
                    project(1, range(0, 4))
                if h == NH + 2:
                    project(0, range(5, 6))
                    project(1, range(4, 6))
            project(0, range(6, NH))
            project(1, range(6, NH))

            keep_clock(WARM[4], 7)
            transposes(3)
            route(1, 2)
            experts(1)

        @block.scalar
        def _(act_e):
            chain = [0]

            def norm(count):
                for t in range(TH):
                    if count == 0:
                        act_e.wait_ge(s_x[t], 16)
                    else:
                        act_e.wait_ge(s_x2, 2 * (count - 1) + t + 1)
                    one = slice(t, t + 1)
                    act_e.activation(h_sb[:, t, :], x_sb[:, t, :], ACT.Square, accum_out=ssq[:, one]).then_inc(s_ssq, 1)
                    act_e.wait_ge(s_ssq, 2 * count + t + 1)
                    chain[0] += 1
                    act_e.activation(root_x[:, one], ssq[:, one], ACT.Ln, scale=1.0 / D, bias=eps_x).then_inc(s_a, 1)
                    act_e.wait_ge(s_a, chain[0])
                    act_e.activation(root_x[:, one], root_x[:, one], ACT.Exp, scale=-0.5).then_inc(s_root, 1)

            def copy_hT(number):
                for t in range(TH):
                    act_e.wait_ge(s_tr, 4 * number + 2 * t + 1)
                    act_e.copy(hT[:, 0:4, t * P:(t + 1) * P], ps[:, 2 * t, :].rearrange("p (k s) -> p k s", k=4))\
                         .then_inc(s_hT[1], 1)

            def group(s, g):
                def gathered(k):
                    act_e.wait_ge(s["xg"], g * E4 + (k + 1))
                    act_e.copy(xg[:, :, :], xg_ps).then_inc(s["xgc"], 1)

                gathered(0)
                for k in range(E4):
                    n1 = g * E4 + (k + 1)
                    act_e.wait_ge(s["gu"], n1)
                    act_e.activation(sg[:, 0, :, :], gu_ps[:, :, 0, :], ACT.Exp, scale=-1.0).then_inc(s["exp"], 1)
                    if k + 1 < E4:
                        gathered(k + 1)
                    act_e.wait_ge(s["y"], n1)
                    for i in range(4):
                        ins = act_e.copy(y[SB * k:SB * (k + 1), :, 256 * i:256 * (i + 1)],
                                         y_ps[SB * i:SB * (i + 1), :, :])
                    ins.then_inc(s["yc"], 1)

            def experts(layer):
                act_e.wait_ge(s_route, layer + 1)
                with act_e.Fori(0, NGRP) as g:
                    group(main, g + layer * NGRP)
                fb = more[layer]
                most = act_e.value_load(cnt[0:1, NE + NGRP:NE + NGRP + 1], min_val=0, max_val=S)
                with act_e.If(most > CAP):
                    with act_e.Fori(0, PASSES - 1) as m:
                        with act_e.If(most > CAP * m + CAP):
                            with act_e.Fori(0, NGRP) as g:
                                group(fb, m * NGRP + g)

            def route(layer):
                act_e.wait_ge(s_dg, 2 * layer + 1)
                act_e.activation(small[:, 400:408], small[:, 408:416], ACT.Exp).then_inc(s_eg, 1)
                act_e.wait_ge(s_dg, 2 * layer + 2)
                act_e.activation(small[:, 416:418], small[:, 418:420], ACT.Exp).then_inc(s_eg, 1)

            act_e.preload_act_table_set("natural_log_exp_and_others")
            act_e.wait_ge(s_z, 1)
            norm(0)
            for g in (1, 3):
                act_e.wait_ge(s_mix, g + 1)
                act_e.copy(mixT[:, 2 * g:2 * g + 2, :], ps[:, g, :].rearrange("p (m s) -> p m s", m=2))\
                     .then_inc(s_mixT[1], 1)
            norm(1)
            copy_hT(0)
            route(0)
            experts(0)

            norm(2)
            copy_hT(1)
            act_e.wait_ge(s_ls, 1)
            act_e.activation(small[:, 434:436], small[:, 432:434], ACT.Exp).then_inc(s_le, 1)
            for t in range(TH):
                act_e.wait_ge(s_vp, t + 1)
                act_e.copy(v_sb[:, t, 0:512], ps[:, 2 * t, :]).then_inc(s_vs[1], 1)

            def copy_queries_keys(h):
                act_e.wait_ge(s_q, h + 1)
                act_e.mul(qT[:, h, :], ps[:, h % 2, 0:S], HD ** -0.5)
                act_e.copy(kT[:, h, :], ps[:, h % 2, S:2 * S]).then_inc(s_qc, 1)

            def copy_weights(h):
                act_e.wait_ge(s_aT, h + 1)
                act_e.copy(aT[:, h % 2, :], ps[:, 4 + 3 * (h % 2), 0:LW]).then_inc(s_aTc, 1)

            def output_root(h):
                act_e.wait_ge(s_o, h + 1)
                if h >= 1:
                    act_e.wait_ge(s_os, h)
                for t in range(TH):
                    chain[0] += 1
                    act_e.activation(junk_o[:, t, :], ps[:, 5 + h % 2, t * P:(t + 1) * P], ACT.Square,
                                     accum_out=small[:, 460 + t:461 + t]).then_inc(s_a, 1)
                act_e.wait_ge(s_a, chain[0])
                act_e.activation(small[:, 462:464], small[:, 460:462], ACT.Ln, scale=1.0 / (2 * HD), bias=eps_o)\
                     .then_inc(s_osq, 1)
                act_e.wait_ge(s_osq, h + 1)
                act_e.activation(small[:, 464:466], small[:, 462:464], ACT.Exp, scale=-0.5).then_inc(s_oroot, 1)

            def exponentials(h):
                act_e.wait_ge(s_m, 4 * (h + 1))
                for c in range(2):
                    for t, cols in ((0, slice(0, P)), (1, slice(P, LW))):
                        at = 440 + 8 * (h % 2) + 2 * c + t
                        act_e.activation(prob[:, h % 2, c, cols], prob[:, h % 2, c, cols], ACT.Exp,
                                         bias=small[:, at:at + 1], accum_out=small[:, at + 4:at + 5]).then_inc(s_ex, 1)

            def copy_output(h):
                act_e.wait_ge(s_oT, h + 1)
                act_e.copy(qT[:, h, :], ps[:, 5 + h % 2, S:2 * S]).then_inc(s_oTc, 1)

            for h in range(NH + 4):
                if h < NH:
                    copy_queries_keys(h)
                if 2 <= h <= NH + 1:
                    copy_weights(h - 2)
                if 3 <= h <= NH + 2:
                    output_root(h - 3)
                if 1 <= h <= NH:
                    exponentials(h - 1)
                if 4 <= h:
                    copy_output(h - 4)
            norm(3)
            copy_hT(2)
            route(1)
            experts(1)
            norm(4)

        @block.vector
        def _(ve):
            chain = [0]

            def then(ins):
                chain[0] += 1
                ins.then_inc(s_v, 1)
                ve.wait_ge(s_v, chain[0])

            def newton(root, mean, factor):
                then(ve.tensor_tensor(factor, root, root, ALU.mult))
                then(ve.tensor_tensor(factor, factor, mean, ALU.mult))
                then(ve.tensor_scalar(factor, factor, -0.5, 1.5, ALU.mult, ALU.add))
                then(ve.tensor_tensor(root, root, factor, ALU.mult))

            def norm(count, g, permuted):
                for t in range(TH):
                    one = slice(t, t + 1)
                    ve.wait_ge(s_ssq, 2 * count + t + 1)
                    then(ve.tensor_scalar(mean_x[:, one], ssq[:, one], 1.0 / D, RMS_EPS, ALU.mult, ALU.add))
                    ve.wait_ge(s_root, 2 * count + t + 1)
                    newton(root_x[:, one], mean_x[:, one], newt_x[:, one])
                    o, a, gg = h_sb[:, t, :], x_sb[:, t, :], g
                    if permuted:
                        o = o.rearrange("p (k q) -> p q k", k=KT)
                        a = a.rearrange("p (q k) -> p q k", k=KT)
                        gg = g.rearrange("p (q k) -> p q k", k=KT)
                    ve.scalar_tensor_tensor(o, a, root_x[:, one], gg, ALU.mult, ALU.mult).then_inc(s_h, 1)

            def copy_hT(number):
                for t in range(TH):
                    ve.wait_ge(s_tr, 4 * number + 2 * t + 2)
                    ve.tensor_copy(hT[:, 4:8, t * P:(t + 1) * P], ps[:, 2 * t + 1, :].rearrange("p (k s) -> p k s", k=4))\
                      .then_inc(s_hT[0], 1)

            def sm(at, *shape):
                n = int(np.prod(shape))
                v = small[:, at:at + n]
                return v if len(shape) == 1 else v.rearrange("p (a b) -> p a b", a=shape[0])

            def wide(v, n):
                return v.unsqueeze(2).to_broadcast([P, v.shape[1], n])

            def numbers(n):
                return iota[:, 0:n].unsqueeze(1).to_broadcast([P, TH, n])

            def first_max(vals, n, top, hit, index, one):
                then(ve.tensor_reduce(top, vals, AX, ALU.max))
                then(ve.tensor_tensor(hit, vals, wide(top, n), ALU.is_ge))
                then(ve.scalar_tensor_tensor(hit, hit, -BIG, numbers(n), ALU.mult, ALU.add))
                then(ve.tensor_reduce(index, hit, AX, ALU.min))
                then(ve.tensor_scalar(index, index, BIG, None, ALU.add))
                then(ve.tensor_tensor(one, numbers(n), wide(index, n), ALU.is_equal))

            def route(layer):
                L = sm(192, TH, NR)
                hit = sm(264, TH, NE)
                M = sm(328, TH, NE)
                gtop, gidx, gone = sm(392, TH), sm(394, TH), sm(424, TH, NG)
                dg = sm(408, TH, NG)
                d2 = sm(418, TH)
                v1, v2, idx = sm(480, TH), sm(482, TH), sm(484, TH)
                one1, one2 = sm(512, TH, NE), sm(576, TH, NE)
                ve.wait_ge(s_lg, layer + 1)
                if layer == 0:
                    ve.wait_ge(s_rb, 64)
                then(ve.tensor_tensor(L, ps[:, 5, 0:128].rearrange("p (t n) -> p t n", t=TH)[:, :, 0:NR],
                                      rb[:, layer, :].unsqueeze(1).to_broadcast([P, TH, NR]), ALU.add))
                first_max(L[:, :, 0:NG], NG, gtop, hit[:, :, 0:NG], gidx, gone)
                then(ve.tensor_tensor(dg, L[:, :, 0:NG], wide(gtop, NG), ALU.subtract))
                ve.sem_inc(s_dg, 1)
                then(ve.tensor_scalar(gone, gone, -1.0, PEN, ALU.add, ALU.mult))
                for t in range(TH):
                    then(ve.tensor_tensor(M[:, t, :].rearrange("p (g e) -> p g e", g=NG),
                                          L[:, t, NG:NR].rearrange("p (g e) -> p g e", g=NG),
                                          wide(gone[:, t, :], EPG), ALU.add))
                first_max(M, NE, v1, hit, idx, one1)
                then(ve.scalar_tensor_tensor(M, one1, -3 * PEN, M, ALU.mult, ALU.add))
                first_max(M, NE, v2, hit, idx, one2)
                then(ve.tensor_tensor(d2, v2, v1, ALU.subtract))
                ve.sem_inc(s_dg, 1)
                then(ve.tensor_tensor(A[:, :, :], one1, one2, ALU.add))
                ve.sem_inc(s_A, 1)
                ve.wait_ge(s_rk, layer + 1)
                then(ve.scalar_tensor_tensor(R[:, :, 0:NE], ps[:, 6, 0:2 * NE].rearrange("p (t e) -> p t e", t=TH), 1.0,
                                             A[:, :, :], ALU.add, ALU.mult))
                then(ve.tensor_scalar(R[:, :, 0:NE], R[:, :, 0:NE], -1.0, None, ALU.add))
                counts, most = sm(640, NE), sm(640 + NE, NGRP)
                then(ve.tensor_copy(counts, ps[:, 6, 2 * NE:3 * NE]))
                then(ve.tensor_reduce(most, counts.rearrange("p (g e) -> p g e", g=NGRP), AX, ALU.max))
                then(ve.tensor_reduce(sm(640 + NE + NGRP, 1), most, AX, ALU.max))
                then(ve.tensor_copy(cnt[:, :], sm(640, NE + NGRP + 1)))
                if layer == 0:
                    then(ve.memset(ps[:, 5:8, :], 0.0))
                ve.sem_inc(s_route, 1)
            def gates(layer):
                eg, e2 = sm(400, TH, NG), sm(416, TH)
                gs, den, w1, w2 = sm(486, TH), sm(490, TH), sm(492, TH), sm(494, TH)
                one1, one2 = sm(512, TH, NE), sm(576, TH, NE)
                ve.wait_ge(s_eg, 2 * layer + 1)
                then(ve.tensor_reduce(gs, eg, AX, ALU.add))
                ve.wait_ge(s_eg, 2 * layer + 2)
                then(ve.tensor_scalar(den, e2, 1.0, None, ALU.add))
                then(ve.tensor_tensor(den, den, gs, ALU.mult))
                then(ve.reciprocal(w1, den))
                then(ve.tensor_tensor(w2, w1, e2, ALU.mult))
                then(ve.tensor_tensor(one1, one1, wide(w1, NE), ALU.mult))
                then(ve.tensor_tensor(one2, one2, wide(w2, NE), ALU.mult))
                then(ve.tensor_tensor(W[:, :, :], one1, one2, ALU.add))

            def place(s, gl):
                for t in range(TH):
                    ins = ve.tensor_tensor(onehot[:, t, :, :, :],
                                           iota.rearrange("p (b s) -> p b s", b=NB).unsqueeze(2).to_broadcast([P, NB, E4, SB]),
                                           R[:, t, bass.ds(gl * E4, E4)].unsqueeze(1).unsqueeze(3).to_broadcast([P, NB, E4, SB]),
                                           ALU.is_equal)
                ins.then_inc(s["onehot"], 1)

            def group(s, g, gl, placed):
                ve.wait_ge(s["onehot"], placed)
                for t in range(TH):
                    ins = ve.tensor_tensor(gated[:, t, :, :, :], onehot[:, t, :, :, :],
                                           W[:, t, bass.ds(gl * E4, E4)].unsqueeze(1).unsqueeze(3).to_broadcast([P, NB, E4, SB]),
                                           ALU.mult)
                ins.then_inc(s["gated"], 1)
                for k in range(E4):
                    n1 = g * E4 + (k + 1)
                    ve.wait_ge(s["exp"], n1)
                    ve.tensor_scalar(sg[:, 1, :, :], sg[:, 0, :, :], 1.0, None, ALU.add).then_inc(s["den"], 1)
                    ve.wait_ge(s["den"], n1)
                    ve.reciprocal(sg[:, 2, :, :], sg[:, 1, :, :]).then_inc(s["sig"], 1)
                    ve.wait_ge(s["sig"], n1)
                    ve.tensor_tensor(sg[:, 3, :, :], sg[:, 2, :, :], gu_ps[:, :, 0, :], ALU.mult).then_inc(s["gh"], 1)
                    ve.wait_ge(s["gh"], n1)
                    ve.tensor_tensor(act[:, :, :], sg[:, 3, :, :], gu_ps[:, :, 1, :], ALU.mult).then_inc(s["act"], 1)
                    ve.wait_ge(s["at"], n1)
                    ve.tensor_copy(actT[:, :, :], at_ps).then_inc(s["atc"], 1)
                ve.wait_ge(s["gt"], g + 1)
                ve.tensor_copy(gateT[:, :, :], gt_ps).then_inc(s["gtc"], 1)
                place(s, gl + 1)

            def experts(layer):
                place(main, 0)
                gates(layer)
                with ve.Fori(0, NGRP) as g:
                    group(main, g + layer * NGRP, g, g + (layer * (NGRP + 1) + 1))
                fb = more[layer]
                most = ve.value_load(cnt[0:1, NE + NGRP:NE + NGRP + 1], min_val=0, max_val=S)
                with ve.If(most > CAP):
                    with ve.Fori(0, PASSES - 1) as m:
                        with ve.If(most > CAP * m + CAP):
                            ve.tensor_scalar(R[:, :, 0:NE], R[:, :, 0:NE], -float(CAP), None, ALU.add).then_inc(fb["shift"], 1)
                            ve.wait_ge(fb["shift"], m + 1)
                            place(fb, 0)
                            with ve.Fori(0, NGRP) as g:
                                group(fb, m * NGRP + g, g, m * (NGRP + 1) + g + 1)
                                ve.wait_ge(fb["sc"], m * NGRP + g + 1)
                ve.wait_ge(main["sc"], NGRP * (layer + 1))
                residual()

            def residual(done=None):
                for t in range(TH):
                    if done is not None:
                        ve.wait_ge(done, t + 1)
                    for i in range(2):
                        xs = x_sb[:, t, 512 * i:512 * (i + 1)]
                        ins = ve.tensor_tensor(xs, xs, ps[:, 2 * t + i, :], ALU.add)
                    ins.then_inc(s_x2, 1)

            ve.memset(eps_x, RMS_EPS)
            ve.memset(eps_o, SUB_EPS)
            then(ve.memset(R[:, :, NE:NE + E4], -1.0))
            ve.memset(zero, 0.0).then_inc(s_z, 1)
            for t in range(TH):
                ve.wait_ge(s_x[t], 16)
            ve.wait_ge(s_mix0, 16)
            norm(0, gain[:, 0, :], False)
            for g in (0, 2):
                ve.wait_ge(s_mix, g + 1)
                ve.tensor_copy(mixT[:, 2 * g:2 * g + 2, :], ps[:, g, :].rearrange("p (m s) -> p m s", m=2))\
                  .then_inc(s_mixT[0], 1)
            ve.wait_ge(s_scale, 16)
            for t in range(TH):
                ve.wait_ge(s_po, t + 1)
                then(ve.tensor_tensor(h_sb[:, t, :], gain[:, 1, :], ps[:, 4 + 2 * t:6 + 2 * t, :].rearrange("p a b -> p (a b)"),
                                      ALU.mult))
                ve.tensor_tensor(x_sb[:, t, :], x_sb[:, t, :], h_sb[:, t, :], ALU.add).then_inc(s_x2, 1)
            ve.wait_ge(s_ffn0, 16)
            norm(1, ffn0, True)
            copy_hT(0)
            ve.wait_ge(s_c, 16)
            route(0)
            experts(0)

            ve.wait_ge(gain_in[0], 16)
            norm(2, gain[:, 0, :], True)
            copy_hT(1)
            ve.wait_ge(s_lam, 80)
            for i in range(2):
                then(ve.tensor_tensor(small[:, 700:764], lam4[:, 2 * i, :], lam4[:, 2 * i + 1, :], ALU.mult))
                then(ve.tensor_reduce(small[:, 432 + i:433 + i], small[:, 700:764], AX, ALU.add))
            ve.sem_inc(s_ls, 1)
            ve.wait_ge(s_le, 1)
            lam = small[:, 436:437]
            then(ve.tensor_tensor(lam, small[:, 434:435], small[:, 435:436], ALU.subtract))
            then(ve.tensor_scalar(lam, lam, LAM_INIT, None, ALU.add))
            then(ve.tensor_scalar(subg[:, :], subg[:, :], 1.0 - LAM_INIT, None, ALU.mult))
            for t in range(TH):
                ve.wait_ge(s_vp, t + 1)
                ve.tensor_copy(v_sb[:, t, 512:1024], ps[:, 2 * t + 1, :]).then_inc(s_vs[0], 1)

            def logits(h):
                ve.wait_ge(s_S, h + 1)
                for c in range(2):
                    ve.scalar_tensor_tensor(prob[:, h % 2, c, :], dist, -(2.0 ** (-8.0 * (h + 1) / NH)),
                                            ps[:, 2 + c, 0:LW], ALU.mult, ALU.add).then_inc(s_L, 1)
                ve.wait_ge(s_L, 2 * (h + 1))
                for c in range(2):
                    for t, cols in ((0, slice(0, P)), (1, slice(P, LW))):
                        at = 440 + 8 * (h % 2) + 2 * c + t
                        ve.tensor_reduce(small[:, at:at + 1], prob[:, h % 2, c, cols], AX, ALU.max, negate=True)\
                          .then_inc(s_m, 1)

            def weights(h):
                ve.wait_ge(s_ex, 4 * (h + 1))
                at = 444 + 8 * (h % 2)
                r = small[:, 770:774]
                then(ve.reciprocal(r, small[:, at:at + 4]))
                then(ve.tensor_scalar(r[:, 2:4], r[:, 2:4], lam, None, ALU.mult))
                for t, cols in ((0, slice(0, P)), (1, slice(P, LW))):
                    ins = ve.tensor_scalar(prob[:, h % 2, 1, cols], prob[:, h % 2, 1, cols], r[:, 2 + t:3 + t], None, ALU.mult)
                then(ins)
                ve.scalar_tensor_tensor(kT[:, h, 0:P], prob[:, h % 2, 0, 0:P], r[:, 0:1], prob[:, h % 2, 1, 0:P],
                                        ALU.mult, ALU.subtract)
                then(ve.scalar_tensor_tensor(qT[:, h, :], prob[:, h % 2, 0, P:LW], r[:, 1:2], prob[:, h % 2, 1, P:LW],
                                             ALU.mult, ALU.subtract))
                ve.sem_inc(s_p, 1)

            def normalise(h):
                ve.wait_ge(s_osq, h + 1)
                then(ve.tensor_scalar(mean_o, small[:, 460:462], 1.0 / (2 * HD), SUB_EPS, ALU.mult, ALU.add))
                ve.wait_ge(s_oroot, h + 1)
                newton(small[:, 464:466], mean_o, newt_o)
                for t in range(TH):
                    ins = ve.scalar_tensor_tensor(h_sb[:, t, h * P:(h + 1) * P], ps[:, 5 + h % 2, t * P:(t + 1) * P],
                                                  small[:, 464 + t:465 + t], subg[:, :], ALU.mult, ALU.mult)
                ins.then_inc(s_os, 1)

            for h in range(1, NH + 3):
                if h <= NH:
                    logits(h - 1)
                if 3 <= h:
                    normalise(h - 3)
                if h <= NH:
                    weights(h - 1)
            residual(s_wo)
            ve.wait_ge(gain_in[1], 16)
            norm(3, gain[:, 1, :], True)
            copy_hT(2)
            route(1)
            experts(1)
            ve.wait_ge(gain_in[0], 32)
            norm(4, gain[:, 0, :], False)


_INS = ["x", "norm_mix_g", "norm_ffn_g", "pool_w", "pool_scale", "attn_wq", "attn_wk", "attn_wv", "attn_wo",
        "attn_lq1", "attn_lk1", "attn_lq2", "attn_lk2", "attn_subln_g", "moe_wg", "moe_bg", "moe_we", "moe_be",
        "moe_w1", "moe_w3", "moe_w2", "final_g"]


def kernel(**inputs):
    import concourse.bacc as bacc
    from concourse.bass_utils import run_bass_kernel_spmd

    nc = bacc.Bacc("TRN2", target_bir_lowering=False, num_devices=1)
    arrays, args = {}, []
    for name in _INS + ["consts"]:
        a = shape_constants() if name == "consts" else np.ascontiguousarray(inputs[name])
        arrays[f"in_{name}"] = a
        args.append(nc.dram_tensor(f"in_{name}", a.shape, mybir.dt.from_np(a.dtype), kind="ExternalInput").ap())
    args.append(nc.dram_tensor("out_x", (1, S, D), F32, kind="ExternalOutput").ap())
    build(nc, *args)
    r = run_bass_kernel_spmd(nc, [arrays], core_ids=[0])
    return r.results[0]["out_x"]
```

```python
import math
from contextlib import ExitStack

import numpy as np

import concourse.bass as bass
from concourse import mybir

F32 = mybir.dt.float32
I32 = mybir.dt.int32
ALU = mybir.AluOpType
ACT = mybir.ActivationFunctionType
AX = mybir.AxisListType.X

P = 128
S, D = 256, 1024
TH = S // P
KT = D // P
NH, HD = 8, 64
NG, EPG = 4, 8
NE = NG * EPG
F = 512
JT = F // P
SB = 32
NB = 2
CAP = SB * NB
PASSES = S // CAP
E4 = P // SB
GPB = 2
BODY = GPB * E4
ITERS = NE // BODY
NGRP = NE // E4
ACC = 4
RING = 8
CH = 4096
CPE = 3
ACH = 8
WINDOWS = (2, 4, 8, 16)
RMS_EPS, SUB_EPS = 1e-6, 1e-5
BIG = 1024.0
PEN = 1e30
LAM_INIT = 0.8 - 0.6 * math.exp(-0.3)
LW = P + S
NR = NG + NE
assert (CPE * NE) % RING == 0 and ACH % RING == 0 and (CPE * BODY) % RING == 0

C_ID, C_U, C_ONE, C_DIST = 0, P, 2 * P, 3 * P
C_IOTA = C_DIST + LW
C_PLACE = C_IOTA + CAP
C_GROUP = C_PLACE + NE
C_BAND = C_GROUP + NE
BW = S + P
C_ALL = C_BAND + len(WINDOWS) * BW


FILL_LOGITS, FILL_RANKS, FILL_ATTN, FILL_LAST = 1, 1, 3, 1


def shape_constants():
    c = np.zeros((P, C_ALL), np.float32)
    i = np.arange(P)
    c[:, C_ID:C_ID + P] = np.eye(P)
    c[:, C_U:C_U + P] = i[:, None] < i[None, :]
    c[:, C_ONE:C_ONE + P] = 1.0
    for half, at, keys in ((0, 0, P), (1, P, S)):
        q, k = i[:, None] + half * P, np.arange(keys)[None, :]
        c[:, C_DIST + at:C_DIST + at + keys] = np.where(k // 64 <= q // 64, np.abs(q - k), 1e33)
    c[:, C_IOTA:C_IOTA + CAP] = np.arange(CAP) + 1
    c[:, C_PLACE:C_PLACE + NE] = np.arange(NE) - BIG
    c[:, C_GROUP:C_GROUP + NE] = np.arange(NE) // EPG - BIG
    for g, win in enumerate(WINDOWS):
        t = np.arange(S)
        lag = t[None, :] - t[:, None]
        band = ((lag >= 0) & (lag < win)) / np.minimum(t + 1, win)[None, :] - (lag == 0)
        at = C_BAND + g * BW
        c[:, at:at + S] = band[:P]
        c[:, at + S:at + BW] = band[P:, P:]
    return c


def build(nc, x, norm_mix_g, norm_ffn_g, pool_w, pool_scale, wq, wk, wv, wo, lq1, lk1, lq2, lk2, subln_g,
          moe_wg, moe_bg, moe_we, moe_be, moe_w1, moe_w3, moe_w2, final_g, consts, out):
    with ExitStack() as ctx:
        def sb(name, shape, dt=F32):
            return ctx.enter_context(nc.sbuf_tensor(name, shape, dt))

        def sem(name):
            return ctx.enter_context(nc.semaphore(name))

        ring = sb("ring", [P, RING, CH])
        x_sb = sb("x_sb", [P, TH, D])
        h_sb = sb("h_sb", [P, TH, D])
        hT = sb("hT", [P, KT, S])
        gain = sb("gain", [P, 2, D])
        cst = sb("cst", [P, C_BAND])
        work = sb("work", [P, 6144])
        work2 = sb("work2", [P, 2304])
        wr = sb("wr", [P, 2, KT, NR])
        rb = sb("rb", [P, 2, NR])
        lam4 = sb("lam4", [P, 4, HD])
        subg = sb("subg", [P, 2 * HD])
        R = sb("R", [P, TH, NE + E4])
        W = sb("W", [P, TH, NE])
        A = sb("A", [P, TH, NE])
        small = sb("small", [P, 1088])
        cnt = sb("cnt", [P, NE + NGRP + 1], I32)
        ident, upper, ones = (cst[:, c:c + P] for c in (C_ID, C_U, C_ONE))
        dist = cst[:, C_DIST:C_DIST + LW]
        iota = cst[:, C_IOTA:C_IOTA + CAP]
        places, group_of = cst[:, C_PLACE:C_PLACE + NE], cst[:, C_GROUP:C_GROUP + NE]

        zero = small[:, 64:64 + P]
        mean_o, newt_o = small[:, 466:468], small[:, 468:470]
        eps_x, eps_o = small[:, 8:9], small[:, 9:10]
        ssq, mean_x, root_x, newt_x = (small[:, c:c + 2] for c in (0, 2, 4, 6))
        junk_o = small[:, 800:1056].rearrange("p (t e) -> p t e", t=TH)
        ffn0 = work2[:, 64:64 + D]
        rows = work2[:, 1280:1280 + D]
        ones_row = small[:, 832:832 + P]
        we_raw = work[:, 5632:6144].rearrange("p (l n) -> p l n", l=2)
        wg_raw = work2[:, 0:64].rearrange("p (l n) -> p l n", l=2)

        band = work[:, 0:len(WINDOWS) * BW]
        pw = work[:, 1536:1536 + 2048].rearrange("p (g c d) -> p g c d", g=4, c=2)
        mixT = work[:, 3584:3584 + 2048].rearrange("p (m s) -> p m s", m=KT)
        qT = work[:, 0:2048].rearrange("p (h s) -> p h s", h=NH)
        kT = work[:, 2048:4096].rearrange("p (h s) -> p h s", h=NH)
        v_sb = work[:, 4096:6144].rearrange("p (t n) -> p t n", t=TH)
        prob = work2[:, 0:4 * LW].rearrange("p (b c w) -> p b c w", b=2, c=2)
        aT = work2[:, 4 * LW:6 * LW].rearrange("p (b w) -> p b w", b=2)
        xg = work[:, 0:512].rearrange("p (k c) -> p k c", k=KT)
        sg = work[:, 512:1536].rearrange("p (m b f) -> p m b f", m=4, b=NB)
        act = work[:, 1536:1792].rearrange("p (b f) -> p b f", b=NB)
        actT = work[:, 1792:2048].rearrange("p (b r) -> p b r", b=NB)
        y = work[:, 2048:4096].rearrange("p (b n) -> p b n", b=NB)
        onehot = work2[:, 0:512].rearrange("p (t b e s) -> p t b e s", t=TH, b=NB, e=E4)
        gated = work2[:, 512:1024].rearrange("p (t b e s) -> p t b e s", t=TH, b=NB, e=E4)
        gateT = work2[:, 1024:1536].rearrange("p (b s) -> p b s", b=NB)

        ps = ctx.enter_context(nc.psum_tensor("ps", [P, 8, 512], F32))
        acc = ps[:, 0:4, :].rearrange("p (t n) w -> p t n w", t=TH)
        xg_ps = ps[:, 4, :].rearrange("p (k c) -> p k c", k=KT)
        gu_ps = ps[:, 5, :].rearrange("p (b m f) -> p b m f", b=NB, m=2)
        gt_ps = ps[:, 4, :].rearrange("p (b s) -> p b s", b=NB)
        y_ps = ps[:, 6, :].rearrange("p (b n) -> p b n", b=NB)
        at_ps = ps[:, 7, 0:256].rearrange("p (b r) -> p b r", b=NB)

        loaded = [sem(f"loaded{i}") for i in range(RING)]
        s_w = sem("s_w")
        s_x = [sem("s_x0"), sem("s_x1")]
        s_c, s_band, s_pw, s_wraw, s_rb, s_lam = (sem(n) for n in ("s_c", "s_band", "s_pw", "s_wraw", "s_rb", "s_lam"))
        s_rows = sem("s_rows")
        s_bc, s_bcc = sem("s_bc"), sem("s_bcc")
        s_wr = sem("s_wr")
        gain_in = [sem("gain_in0"), sem("gain_in1")]
        s_out = sem("s_out")
        s_ssq = sem("s_ssq")
        s_root = sem("s_root")
        s_x2 = sem("s_x2")
        s_h = sem("s_h")
        s_r = sem("s_r")
        s_hn = sem("s_hn")
        s_mix, s_po = sem("s_mix"), sem("s_po")
        s_mixT = [sem("s_mixT_v"), sem("s_mixT_a")]
        s_tr = sem("s_tr")
        s_hT = [sem("s_hT_v"), sem("s_hT_a")]
        s_lg, s_A, s_rk, s_route = sem("s_lg"), sem("s_A"), sem("s_rk"), sem("s_route")
        s_dg, s_eg = sem("s_dg"), sem("s_eg")
        s_v = sem("s_v")
        s_a = sem("s_a")
        s_z = sem("s_z")
        s_vp = sem("s_vp")
        s_vs = [sem("s_vs_v"), sem("s_vs_a")]
        s_q, s_qc = sem("s_q"), sem("s_qc")
        s_k = sem("s_k")
        s_S, s_L, s_ex, s_p = sem("s_S"), sem("s_L"), sem("s_ex"), sem("s_p")
        s_m = sem("s_m")
        s_aT, s_aTc, s_o = sem("s_aT"), sem("s_aTc"), sem("s_o")
        s_osq, s_oroot, s_os = sem("s_osq"), sem("s_oroot"), sem("s_os")
        s_oT, s_oTc, s_wo = sem("s_oT"), sem("s_oTc"), sem("s_wo")
        s_ls, s_le = sem("s_ls"), sem("s_le")

        STEPS = ("onehot", "gated", "xg", "xgc", "half", "gu", "exp", "den", "sig", "gh", "act", "at", "atc", "y", "yc_v", "yc_a",
                 "gt", "gtc", "sc", "shift", "passed", "wl0", "wl1", "wl2")

        def moe_sems(name):
            return {k: sem(f"{name}_{k}") for k in STEPS}

        main = moe_sems("m")
        more = [moe_sems("p0"), moe_sems("p1")]

        def use_before(layer):
            return layer * (CPE * NE + ACH) // RING

        def chunk_parts(layer, e, j):
            if j < 2:
                return [(m * 2048, w[layer, e, :, :].rearrange("(p k) n -> p k n", k=KT)[:, 4 * j:4 * j + 4, :])
                        for m, w in ((0, moe_w1), (1, moe_w3))]
            w = moe_w2[layer, e, :, :].rearrange("(j p) n -> p j n", p=P)
            return [(m * 2048, w[:, 2 * m:2 * m + 2, :]) for m in range(2)]

        def attn_parts(c):
            w = (wv, wq, wk, wo)[c // 2]
            if c < 6:
                w = w[0].rearrange("(p k) n -> p k n", k=KT)
            else:
                w = w[0].rearrange("(k p) n -> p k n", p=P)
            at = 4 * (c % 2)
            return [(m * 2048, w[:, at + 2 * m:at + 2 * m + 2, :]) for m in range(2)]

        def view(src):
            return src.shape[1], src.shape[2]

        block = ctx.enter_context(nc.Block())

        @block.sync
        def _(sp):
            def load(slot, parts, signal):
                for at, src in parts:
                    k, n = view(src)
                    sp.dma_start(ring[:, slot, at:at + k * n].rearrange("p (k n) -> p k n", k=k), src) \
                      .then_inc(signal, 16)

            def row(dst, src):
                return sp.dma_start(dst, src.to_broadcast([P] + list(src.shape[1:])))

            for r, g in enumerate((norm_mix_g[0:1, :], pool_scale[0:1, :], norm_ffn_g[0:1, :], norm_mix_g[1:2, :])):
                sp.dma_start(rows[32 * r:32 * r + 1, :], g).then_inc(s_rows, 16)
            for t in range(TH):
                sp.dma_start(x_sb[:, t, :], x[0, t * P:(t + 1) * P, :]).then_inc(s_x[t], 16)
            sp.dma_start(band, consts[:, C_BAND:C_ALL]).then_inc(s_band, 16)
            sp.dma_start(pw, pool_w[0].rearrange("g (c p) d -> p g c d", p=P)).then_inc(s_pw, 16)
            sp.dma_start(cst[:, :], consts[:, 0:C_BAND]).then_inc(s_c, 16)
            sp.dma_start(wg_raw, moe_wg.rearrange("l (p k) n -> p l (k n)", k=KT)).then_inc(s_wraw, 16)
            sp.dma_start(we_raw, moe_we.rearrange("l (p k) n -> p l (k n)", k=KT)).then_inc(s_wraw, 16)
            for layer in range(2):
                row(rb[:, layer, 0:NG], moe_bg[layer:layer + 1, :]).then_inc(s_rb, 16)
                row(rb[:, layer, NG:NR], moe_be[layer:layer + 1, :]).then_inc(s_rb, 16)
            used = (main["half"], main["gu"], main["y"])
            attn_used = ((s_vp, 2), (s_vp, 2), (s_q, NH), (s_q, NH), (s_q, NH), (s_q, NH), (s_wo, 4), (s_wo, 4))
            for layer in range(2):
                for c in range(RING):
                    if layer == 1:
                        sp.wait_ge(*attn_used[c])
                    load(c, chunk_parts(layer, c // CPE, c % CPE), loaded[c])
                steady = CPE * BODY

                def stream(it, c):
                    e, j = divmod(c - RING, CPE)
                    sp.wait_ge(used[j], it * BODY + (layer * NE + e + 1))
                    load(c % RING, chunk_parts(layer, it * BODY + c // CPE, c % CPE), loaded[c % RING])

                with sp.Fori(0, ITERS - 1) as it:
                    for c in range(RING, RING + steady):
                        stream(it, c)
                for c in range(RING, steady):
                    stream(ITERS - 1, c)
                fb = more[layer]
                sp.wait_ge(s_route, layer + 1)
                most = sp.value_load(cnt[0:1, NE + NGRP:NE + NGRP + 1], min_val=0, max_val=S)
                with sp.If(most > CAP):
                    sp.wait_ge(main["y"], NE * (layer + 1))
                    with sp.Fori(0, PASSES - 1) as m:
                        with sp.If(most > CAP * m + CAP):
                            with sp.Fori(0, NE) as e:
                                n = m * NE + e
                                for j in range(CPE):
                                    load(j, chunk_parts(layer, e, j), fb[f"wl{j}"])
                                sp.wait_ge(fb["y"], n + 1)
                                sp.sem_inc(fb["passed"], 1)
                if layer == 0:
                    for c in range(ACH):
                        e, j = divmod(CPE * NE - RING + c, CPE)
                        sp.wait_ge(used[j], e + 1)
                        load(c, attn_parts(c), loaded[c])
            for t in range(TH):
                sp.wait_ge(s_h, 2 * 4 + t + 1)
                sp.dma_start(out[0, t * P:(t + 1) * P, :], h_sb[:, t, :]).then_inc(s_out, 16)
            sp.wait_ge(s_out, 32)

        @block.gpsimd
        def _(pool):
            def row(dst, src):
                return pool.dma_start(dst, src.to_broadcast([P] + list(src.shape[1:])))

            for i, w in enumerate((lq1, lk1, lq2, lk2)):
                row(lam4[:, i, :], w[0:1, :]).then_inc(s_lam, 16)
            row(subg[:, :], subln_g[0:1, :]).then_inc(s_lam, 16)
            pool.wait_ge(s_wraw, 32)
            for layer in range(2):
                pool.tensor_copy(wr[:, layer, :, 0:NG], wg_raw[:, layer, :].rearrange("p (k n) -> p k n", k=KT)).then_inc(s_wr, 1)
                pool.tensor_copy(wr[:, layer, :, NG:NR], we_raw[:, layer, :].rearrange("p (k n) -> p k n", k=KT)).then_inc(s_wr, 1)
            pool.wait_ge(s_vp, 2)
            row(gain[:, 1, :], norm_ffn_g[1:2, :]).then_inc(gain_in[1], 16)
            pool.wait_ge(s_h, 6)
            row(gain[:, 0, :], final_g.rearrange("(a d) -> a d", a=1)).then_inc(gain_in[0], 16)

        @block.tensor
        def _(pe):
            def transposes(count, t):
                pe.wait_ge(s_h, 2 * count + t + 1)
                for k in range(KT):
                    mm = pe.transpose(ps[:, 2 * t + k // 4, (k % 4) * P:(k % 4 + 1) * P],
                                      h_sb[:, t, k * P:(k + 1) * P], ident)
                    if k % 4 == 3:
                        mm.then_inc(s_tr, 1)

            def keep_clock(products, bank):
                for _ in range(products):
                    pe.matmul(ps[:, bank, :], zero, cst[:, 0:512], start=True, stop=True)

            def broadcast(r, bank):
                p = slice(32 * r, 32 * r + 1)
                for i in range(2):
                    mm = pe.matmul(ps[:, bank + i, :], ones_row[p, :], rows[p, 512 * i:512 * (i + 1)], start=True, stop=True)
                mm.then_inc(s_bc, 1)

            def wait_hT(number, t):
                for s in s_hT:
                    pe.wait_ge(s, 2 * number + t + 1)

            def route(layer, number):
                if layer == 0:
                    pe.wait_ge(s_wr, 4)
                for t in range(TH):
                    if t > 0 and layer == 0:
                        pe.wait_ge(s_bcc, 3)
                    if t > 0 or layer == 0:
                        transposes(2 * layer + 1, t)
                    if t == 0 and layer == 0:
                        pe.wait_ge(s_bcc, 2)
                        broadcast(3, 2)
                    wait_hT(number, t)
                    for k in range(KT):
                        mm = pe.matmul(ps[:, 5, t * 64:t * 64 + NR], hT[:, k, t * P:(t + 1) * P],
                                       wr[:, layer, k, :], start=(k == 0), stop=(k == KT - 1))
                mm.then_inc(s_lg, 1)
                for b in range(ACC):
                    pe.matmul(ps[:, b, :], zero, cst[:, 0:512], start=True, stop=True)
                keep_clock(FILL_LOGITS, 0)
                pe.wait_ge(s_A, layer + 1)
                pe.matmul(ps[:, 6, 0:NE], upper, A[:, 0, :], start=True, stop=True)
                pe.matmul(ps[:, 6, NE:2 * NE], ones, A[:, 0, :], start=True, stop=False)
                pe.matmul(ps[:, 6, NE:2 * NE], upper, A[:, 1, :], start=False, stop=True)
                pe.matmul(ps[:, 6, 2 * NE:3 * NE], ones, A[:, 0, :], start=True, stop=False)
                pe.matmul(ps[:, 6, 2 * NE:3 * NE], ones, A[:, 1, :], start=False, stop=True).then_inc(s_rk, 1)
                keep_clock(FILL_RANKS, 0)
                
            def group(s, g, placed, routed, fullest, tokens, chunk):
                def by_count(count, step):
                    if count is None:
                        step(NB)
                    else:
                        with pe.If(count > SB):
                            step(NB)
                        with pe.Else():
                            step(1)

                def gather(k):
                    for kt in range(KT):
                        for t in range(TH):
                            mm = pe.matmul(xg_ps[:, kt, :], h_sb[:, t, kt * P:(kt + 1) * P],
                                           onehot[:, t, :, k, :], start=(t == 0), stop=(t == TH - 1))
                    mm.then_inc(s["xg"], 1)

                def expert(k, blocks):
                    n1 = g * E4 + k + 1
                    for half in range(2):
                        if half == 0:
                            pe.wait_ge(s["xgc"], n1)
                        w = ring[:, chunk(k, half), :].rearrange("p (m k n) -> p m k n", m=2, k=4)
                        for b in reversed(range(blocks)):
                            for q in range(4):
                                for j in range(JT):
                                    mm = pe.matmul(gu_ps[SB * j:SB * (j + 1), b, :, :],
                                                   xg[:, 4 * half + q, SB * b:SB * (b + 1)],
                                                   w[:, :, q, P * j:P * (j + 1)],
                                                   start=(half == 0 and q == 0 and b == blocks - 1),
                                                   stop=(half == 1 and q == 3), skip_group_check=True)
                        mm.then_inc(s["half"] if half == 0 else s["gu"], 1)
                    if k + 1 < E4:
                        gather(k + 1)
                    else:
                        pe.wait_ge(s["gated"], g + 1)
                        for b in range(NB):
                            for t in range(TH):
                                mm = pe.transpose(gt_ps[:, b, t * P:(t + 1) * P],
                                                  gated[:, t, b, :, :].rearrange("p e s -> p (e s)"), ident)
                        mm.then_inc(s["gt"], 1)
                        keep_clock(FILL_LAST, 7)
                    pe.wait_ge(s["act"], n1)
                    for b in range(blocks):
                        mm = pe.transpose(at_ps[:, b, :], act[:, b, :], ident)
                    mm.then_inc(s["at"], 1)
                    pe.wait_ge(s["atc"], n1)
                    if k > 0:
                        for half in ("yc_v", "yc_a"):
                            pe.wait_ge(s[half], n1 - 1)
                    w = ring[:, chunk(k, 2), :].rearrange("p (j n) -> p j n", j=JT)
                    for b in range(blocks):
                        for j in range(JT):
                            for i in range(4):
                                mm = pe.matmul(y_ps[SB * i:SB * (i + 1), b, :], actT[:, b, SB * j:SB * (j + 1)],
                                               w[:, j, 256 * i:256 * (i + 1)], start=(j == 0), stop=(j == JT - 1))
                    mm.then_inc(s["y"], 1)
                    if k == E4 - 1:
                        keep_clock(FILL_LAST, 7)

                def scatter(blocks):
                    for t in range(TH):
                        for i in range(2):
                            for b in range(blocks):
                                mm = pe.matmul(acc[:, t, i, :], gateT[:, b, t * P:(t + 1) * P],
                                               y[:, b, 512 * i:512 * (i + 1)], start=False, stop=False,
                                               skip_group_check=True)
                            mm.then_inc(s["sc"], 1)

                pe.wait_ge(s["onehot"], placed)
                gather(0)
                pe.wait_ge(s_route, routed)
                for k in range(E4):
                    count = tokens(k)
                    by_count(count, lambda blocks, k=k: expert(k, blocks))
                most = fullest()
                pe.wait_ge(s["gtc"], g + 1)
                for half in ("yc_v", "yc_a"):
                    pe.wait_ge(s[half], g * E4 + E4)
                by_count(most, scatter)

            def experts(layer):
                u0 = use_before(layer)
                pe.wait_ge(s_hn, 2 * (layer + 1))
                with pe.Fori(0, ITERS) as it:
                    for gg in range(GPB):
                        g = it * GPB + (layer * NGRP + gg)

                        def fullest(gg=gg):
                            return pe.value_load(cnt[0:1, bass.ds(it * GPB + (NE + gg), 1)], min_val=0, max_val=S)

                        def tokens(k, gg=gg):
                            return pe.value_load(cnt[0:1, bass.ds(it * BODY + (gg * E4 + k), 1)], min_val=0, max_val=S)

                        def chunk(k, j, gg=gg):
                            c = CPE * (gg * E4 + k) + j
                            pe.wait_ge(loaded[c % RING], (it * (CPE * BODY // RING) + (u0 + c // RING + 1)) * 32)
                            return c % RING

                        group(main, g, it * GPB + (layer * (NGRP + 1) + gg + 1), layer + 1, fullest, tokens, chunk)
                fb = more[layer]
                most = pe.value_load(cnt[0:1, NE + NGRP:NE + NGRP + 1], min_val=0, max_val=S)
                with pe.If(most > CAP):
                    with pe.Fori(0, PASSES - 1) as m:
                        with pe.If(most > CAP * m + CAP):
                            with pe.Fori(0, NGRP) as gg:
                                g = m * NGRP + gg

                                def chunk(k, j):
                                    pe.wait_ge(fb[f"wl{j}"], (g * E4 + (k + 1)) * 32)
                                    return j

                                group(fb, g, m * (NGRP + 1) + gg + 1, layer + 1, lambda: None, lambda k: None, chunk)

            pe.wait_ge(s_z, 1)
            pe.wait_ge(s_rows, 64)
            broadcast(0, 4)
            broadcast(1, 6)

            pe.wait_ge(s_h, 2)
            pe.wait_ge(s_band, 16)
            for m in range(KT):
                at = (m // 2) * BW
                o = ps[:, m // 2, (m % 2) * S:(m % 2 + 1) * S]
                pe.matmul(o, h_sb[:, 0, m * P:(m + 1) * P], band[:, at:at + S], start=True, stop=False)
                mm = pe.matmul(o[:, P:S], h_sb[:, 1, m * P:(m + 1) * P], band[:, at + S:at + BW], start=False, stop=True)
                if m % 2 == 1:
                    mm.then_inc(s_mix, 1)
            pe.wait_ge(s_pw, 16)
            for t in range(TH):
                if t == 1:
                    broadcast(2, 2)
                    pe.wait_ge(s_bcc, 1)
                for g in range(4):
                    if t == 0:
                        pe.wait_ge(s_mixT[g % 2], g // 2 + 1)
                    for c in range(2):
                        mm = pe.matmul(ps[:, 4 + 2 * t + g // 2, (g % 2) * S:(g % 2 + 1) * S],
                                       mixT[:, 2 * g + c, t * P:(t + 1) * P], pw[:, g, c, :],
                                       start=(c == 0), stop=(c == 1))
                mm.then_inc(s_po, 1)
            pe.wait_ge(s_c, 16)
            route(0, 0)
            experts(0)

            keep_clock(FILL_ATTN, 7)
            transposes(2, 0)
            u = CPE * NE // RING + 1

            def matrix(c, kt):
                return ring[:, c + kt // 4, :].rearrange("p (k n) -> p k n", k=4)[:, kt % 4, :]

            for t in range(TH):
                wait_hT(1, t)
                for kt in range(KT):
                    if t == 0 and kt % 4 == 0:
                        pe.wait_ge(loaded[kt // 4], 32 * u)
                    if t == 0 and kt == KT - 2:
                        transposes(2, 1)
                    for i in range(2):
                        mm = pe.matmul(ps[:, 2 * t + i, :], hT[:, kt, t * P:(t + 1) * P],
                                       matrix(0, kt)[:, 512 * i:512 * (i + 1)], start=(kt == 0), stop=(kt == KT - 1))
                mm.then_inc(s_vp, 1)

            def queries_keys(h):
                if h < 2:
                    pe.wait_ge(s_vs[1 - h], 1)
                else:
                    pe.wait_ge(s_qc, h - 1)
                for i in range(2):
                    for kt in range(KT):
                        if h == 0 and kt % 4 == 0:
                            pe.wait_ge(loaded[2 + 2 * i + kt // 4], 32 * u)
                        mm = pe.matmul(ps[:, h % 2, i * S:(i + 1) * S], matrix(2 + 2 * i, kt)[:, h * P:(h + 1) * P],
                                       hT[:, kt, :], start=(kt == 0), stop=(kt == KT - 1))
                mm.then_inc(s_q, 1)

            def scores(h):
                pe.wait_ge(s_qc, h + 1)
                if h == 0:
                    for s in s_vs:
                        pe.wait_ge(s, 2)
                else:
                    pe.wait_ge(s_L, 2 * h)
                for queries, keys in ((slice(0, P), slice(0, P)), (slice(P, S), slice(0, S))):
                    for c in range(2):
                        r = slice(HD * c, HD * (c + 1))
                        cols = slice(queries.start, queries.start + keys.stop)
                        mm = pe.matmul(ps[:, 2 + c, cols], qT[r, h, queries], kT[r, h, keys], start=True, stop=True)
                mm.then_inc(s_S, 1)

            def turn_weights(h):
                pe.wait_ge(s_p, h + 1)
                if h >= 2:
                    pe.wait_ge(s_aTc, h - 1)
                bank = ps[:, 4 + 3 * (h % 2), :]
                pe.transpose(bank[:, 0:P], kT[:, h, 0:P], ident)
                pe.transpose(bank[:, P:2 * P], qT[:, h, 0:P], ident)
                pe.transpose(bank[:, 2 * P:3 * P], qT[:, h, P:S], ident).then_inc(s_aT, 1)

            def attend(h):
                pe.wait_ge(s_aTc, h + 1)
                if h >= 2:
                    pe.wait_ge(s_oTc, h - 1)
                bank, e = ps[:, 5 + h % 2, :], slice(h * P, (h + 1) * P)
                pe.matmul(bank[:, 0:P], aT[:, h % 2, 0:P], v_sb[:, 0, e], start=True, stop=True)
                pe.matmul(bank[:, P:S], aT[:, h % 2, P:2 * P], v_sb[:, 0, e], start=True, stop=False)
                pe.matmul(bank[:, P:S], aT[:, h % 2, 2 * P:3 * P], v_sb[:, 1, e], start=False, stop=True)\
                  .then_inc(s_o, 1)

            def turn_output(h):
                pe.wait_ge(s_os, h + 1)
                for t in range(TH):
                    mm = pe.transpose(ps[:, 5 + h % 2, S + t * P:S + (t + 1) * P], h_sb[:, t, h * P:(h + 1) * P], ident)
                mm.then_inc(s_oT, 1)

            def project(t, heads):
                for h in heads:
                    if h % 4 == 0:
                        pe.wait_ge(loaded[6 + h // 4], 32 * u)
                    pe.wait_ge(s_oTc, h + 1)
                    for i in range(2):
                        mm = pe.matmul(ps[:, 2 * t + i, :], qT[:, h, t * P:(t + 1) * P],
                                       matrix(6, h)[:, 512 * i:512 * (i + 1)], start=(h == 0), stop=(h == NH - 1))
                        if h == NH - 1:
                            mm.then_inc(s_wo, 1)

            for h in range(NH + 4):
                if h < NH:
                    queries_keys(h)
                if 1 <= h <= NH:
                    scores(h - 1)
                if h == NH:
                    project(0, range(0, 2))
                if 2 <= h <= NH + 1:
                    turn_weights(h - 2)
                if 3 <= h <= NH + 2:
                    attend(h - 3)
                if 4 <= h:
                    turn_output(h - 4)
                if h == NH:
                    project(0, range(2, 4))
                if h == NH + 1:
                    project(0, range(4, 5))
                    pe.wait_ge(s_L, 2 * NH)
                    project(1, range(0, 1))
                if h == NH + 2:
                    project(0, range(5, 6))
                    project(1, range(1, 2))
            project(1, range(2, 3))
            project(0, range(6, NH))
            project(1, range(3, NH - 1))
            transposes(3, 0)
            project(1, range(NH - 1, NH))

            route(1, 2)
            experts(1)

        @block.scalar
        def _(act_e):
            chain = [0]

            def norm(count, t, squares=None):
                squares = h_sb[:, t, :] if squares is None else squares
                if count == 0:
                    act_e.wait_ge(s_x[t], 16)
                else:
                    act_e.wait_ge(s_x2, 2 * (count - 1) + t + 1)
                one = slice(t, t + 1)
                act_e.activation(squares, x_sb[:, t, :], ACT.Square, accum_out=ssq[:, one]).then_inc(s_ssq, 1)
                act_e.wait_ge(s_ssq, 2 * count + t + 1)
                chain[0] += 1
                act_e.activation(root_x[:, one], ssq[:, one], ACT.Ln, scale=1.0 / D, bias=eps_x).then_inc(s_a, 1)
                act_e.wait_ge(s_a, chain[0])
                act_e.activation(root_x[:, one], root_x[:, one], ACT.Exp, scale=-0.5).then_inc(s_root, 1)

            def copy_hT(number, t):
                act_e.wait_ge(s_tr, 4 * number + 2 * t + 1)
                act_e.copy(hT[:, 0:4, t * P:(t + 1) * P], ps[:, 2 * t, :].rearrange("p (k s) -> p k s", k=4))\
                     .then_inc(s_hT[1], 1)

            def group(s, g):
                def gathered(k):
                    act_e.wait_ge(s["xg"], g * E4 + (k + 1))
                    act_e.copy(xg[:, :, :], xg_ps).then_inc(s["xgc"], 1)

                gathered(0)
                for k in range(E4):
                    n1 = g * E4 + (k + 1)
                    act_e.wait_ge(s["gu"], n1)
                    act_e.activation(sg[:, 0, :, :], gu_ps[:, :, 0, :], ACT.Exp, scale=-1.0).then_inc(s["exp"], 1)
                    if k + 1 < E4:
                        gathered(k + 1)
                    else:
                        act_e.wait_ge(s["gt"], g + 1)
                        act_e.copy(gateT[:, :, :], gt_ps).then_inc(s["gtc"], 1)
                    act_e.wait_ge(s["y"], n1)
                    for i in (2, 3):
                        ins = act_e.copy(y[SB * k:SB * (k + 1), :, 256 * i:256 * (i + 1)],
                                         y_ps[SB * i:SB * (i + 1), :, :])
                    ins.then_inc(s["yc_a"], 1)

            def experts(layer):
                act_e.wait_ge(s_route, layer + 1)
                with act_e.Fori(0, NGRP) as g:
                    group(main, g + layer * NGRP)
                fb = more[layer]
                most = act_e.value_load(cnt[0:1, NE + NGRP:NE + NGRP + 1], min_val=0, max_val=S)
                with act_e.If(most > CAP):
                    with act_e.Fori(0, PASSES - 1) as m:
                        with act_e.If(most > CAP * m + CAP):
                            with act_e.Fori(0, NGRP) as g:
                                group(fb, m * NGRP + g)

            def route(layer):
                act_e.wait_ge(s_dg, 2 * layer + 1)
                act_e.activation(small[:, 400:408], small[:, 408:416], ACT.Exp).then_inc(s_eg, 1)
                act_e.wait_ge(s_dg, 2 * layer + 2)
                act_e.activation(small[:, 416:418], small[:, 418:420], ACT.Exp).then_inc(s_eg, 1)

            act_e.preload_act_table_set("natural_log_exp_and_others")
            act_e.wait_ge(s_z, 1)
            for t in range(TH):
                norm(0, t)

            def copy_gain(number, dst, bank):
                act_e.wait_ge(s_bc, number)
                act_e.copy(dst, ps[:, bank:bank + 2, :].rearrange("p a b -> p (a b)")).then_inc(s_bcc, 1)

            copy_gain(2, gain[:, 1, :], 6)
            for g in (1, 3):
                act_e.wait_ge(s_mix, g + 1)
                act_e.copy(mixT[:, 2 * g:2 * g + 2, :], ps[:, g, :].rearrange("p (m s) -> p m s", m=2))\
                     .then_inc(s_mixT[1], 1)
            def normalise_tokens(layer, t):
                act_e.wait_ge(s_r, 2 * layer + t + 1)
                act_e.wait_ge(s_tr, 8 * layer + 2 * t + 2)
                act_e.mul(h_sb[:, t, :], h_sb[:, t, :], root_x[:, t:t + 1]).then_inc(s_hn, 1)

            copy_gain(3, ffn0, 2)
            for t in range(TH):
                norm(1, t, work[:, 0:D])
                copy_hT(0, t)
                normalise_tokens(0, t)
                if t == 0:
                    copy_gain(4, gain[:, 0, :], 2)
            route(0)
            experts(0)

            for t in range(TH):
                norm(2, t)
                copy_hT(1, t)
            act_e.wait_ge(s_ls, 1)
            act_e.activation(small[:, 434:436], small[:, 432:434], ACT.Exp).then_inc(s_le, 1)
            for t in range(TH):
                act_e.wait_ge(s_vp, t + 1)
                act_e.copy(v_sb[:, t, 0:512], ps[:, 2 * t, :]).then_inc(s_vs[1], 1)

            def copy_queries_keys(h):
                act_e.wait_ge(s_q, h + 1)
                act_e.mul(qT[:, h, :], ps[:, h % 2, 0:S], HD ** -0.5)
                act_e.copy(kT[:, h, :], ps[:, h % 2, S:2 * S]).then_inc(s_qc, 1)

            def copy_weights(h):
                act_e.wait_ge(s_aT, h + 1)
                act_e.copy(aT[:, h % 2, :], ps[:, 4 + 3 * (h % 2), 0:LW]).then_inc(s_aTc, 1)

            def output_root(h):
                act_e.wait_ge(s_o, h + 1)
                if h >= 1:
                    act_e.wait_ge(s_os, h)
                for t in range(TH):
                    chain[0] += 1
                    act_e.activation(junk_o[:, t, :], ps[:, 5 + h % 2, t * P:(t + 1) * P], ACT.Square,
                                     accum_out=small[:, 460 + t:461 + t]).then_inc(s_a, 1)
                act_e.wait_ge(s_a, chain[0])
                act_e.activation(small[:, 462:464], small[:, 460:462], ACT.Ln, scale=1.0 / (2 * HD), bias=eps_o)\
                     .then_inc(s_osq, 1)
                act_e.wait_ge(s_osq, h + 1)
                act_e.activation(small[:, 464:466], small[:, 462:464], ACT.Exp, scale=-0.5).then_inc(s_oroot, 1)

            def exponentials(h):
                act_e.wait_ge(s_m, 4 * (h + 1))
                for c in range(2):
                    for t, cols in ((0, slice(0, P)), (1, slice(P, LW))):
                        at = 440 + 8 * (h % 2) + 2 * c + t
                        act_e.activation(prob[:, h % 2, c, cols], prob[:, h % 2, c, cols], ACT.Exp,
                                         bias=small[:, at:at + 1], accum_out=small[:, at + 4:at + 5]).then_inc(s_ex, 1)

            def copy_output(h):
                act_e.wait_ge(s_oT, h + 1)
                act_e.copy(qT[:, h, :], ps[:, 5 + h % 2, S:2 * S]).then_inc(s_oTc, 1)

            for h in range(NH + 4):
                if h < NH:
                    copy_queries_keys(h)
                if 2 <= h <= NH + 1:
                    copy_weights(h - 2)
                if 3 <= h <= NH + 2:
                    output_root(h - 3)
                if 1 <= h <= NH:
                    exponentials(h - 1)
                if 4 <= h:
                    copy_output(h - 4)
            for t in range(TH):
                norm(3, t, work[:, 4096:4096 + D])
                copy_hT(2, t)
                normalise_tokens(1, t)
            route(1)
            experts(1)
            for t in range(TH):
                norm(4, t)

        @block.vector
        def _(ve):
            chain = [0]

            def then(ins):
                chain[0] += 1
                ins.then_inc(s_v, 1)
                ve.wait_ge(s_v, chain[0])

            def newton(root, mean, factor):
                if root.shape[1] == 1:
                    then(ve.scalar_tensor_tensor(factor, root, mean, root, ALU.mult, ALU.mult))
                else:
                    then(ve.tensor_tensor(factor, root, root, ALU.mult))
                    then(ve.tensor_tensor(factor, factor, mean, ALU.mult))
                then(ve.scalar_tensor_tensor(root, factor, 1.5, root, ALU.add, ALU.mult))

            def root(count, t):
                one = slice(t, t + 1)
                ve.wait_ge(s_ssq, 2 * count + t + 1)
                then(ve.tensor_scalar(mean_x[:, one], ssq[:, one], -0.5 / D, -0.5 * RMS_EPS, ALU.mult, ALU.add))
                ve.wait_ge(s_root, 2 * count + t + 1)
                newton(root_x[:, one], mean_x[:, one], newt_x[:, one])

            def operands(t, g, permuted):
                o, a = h_sb[:, t, :], x_sb[:, t, :]
                if permuted:
                    o = o.rearrange("p (k q) -> p q k", k=KT)
                    a = a.rearrange("p (q k) -> p q k", k=KT)
                    g = g.rearrange("p (q k) -> p q k", k=KT)
                return o, a, g

            def norm(count, t, g, permuted):
                root(count, t)
                o, a, gg = operands(t, g, permuted)
                ve.scalar_tensor_tensor(o, a, root_x[:, t:t + 1], gg, ALU.mult, ALU.mult).then_inc(s_h, 1)

            def router_norm(count, t, g):
                ve.wait_ge(s_x2, 2 * (count - 1) + t + 1)
                o, a, gg = operands(t, g, True)
                ve.tensor_tensor(o, a, gg, ALU.mult).then_inc(s_h, 1)
                root(count, t)
                ve.sem_inc(s_r, 1)

            def copy_hT(number, t):
                ve.wait_ge(s_tr, 4 * number + 2 * t + 2)
                ve.tensor_copy(hT[:, 4:8, t * P:(t + 1) * P], ps[:, 2 * t + 1, :].rearrange("p (k s) -> p k s", k=4))\
                  .then_inc(s_hT[0], 1)

            def sm(at, *shape):
                n = int(np.prod(shape))
                v = small[:, at:at + n]
                return v if len(shape) == 1 else v.rearrange("p (a b) -> p a b", a=shape[0])

            def wide(v, n):
                return v.unsqueeze(2).to_broadcast([P, v.shape[1], n])

            def numbers(n):
                return places[:, 0:n].unsqueeze(1).to_broadcast([P, TH, n])

            def first_max(vals, n, top, hit, index):
                then(ve.tensor_reduce(top, vals, AX, ALU.max))
                for t in range(TH):
                    ins = ve.scalar_tensor_tensor(hit[:, t, :], vals[:, t, :], top[:, t:t + 1], places[:, 0:n],
                                                  ALU.is_ge, ALU.mult)
                then(ins)
                then(ve.tensor_reduce(index, hit, AX, ALU.min))

            def route(layer):
                L = sm(192, TH, NR)
                hit = sm(264, TH, NE)
                M = sm(328, TH, NE)
                gtop, gidx = sm(392, TH), sm(394, TH)
                dg = sm(408, TH, NG)
                d2 = sm(418, TH)
                v1, v2, idx1, idx2 = sm(480, TH), sm(482, TH), sm(484, TH), sm(496, TH)
                one1, one2 = sm(512, TH, NE), sm(576, TH, NE)
                ve.wait_ge(s_lg, layer + 1)
                if layer == 0:
                    ve.wait_ge(s_rb, 64)
                for t in range(TH):
                    ins = ve.scalar_tensor_tensor(L[:, t, :], ps[:, 5, t * 64:t * 64 + NR], root_x[:, t:t + 1],
                                                  rb[:, layer, :], ALU.mult, ALU.add)
                then(ins)
                first_max(L[:, :, 0:NG], NG, gtop, hit[:, :, 0:NG], gidx)
                for t in range(TH):
                    ins = ve.tensor_scalar(M[:, t, :], group_of, gidx[:, t:t + 1], -PEN, ALU.not_equal, ALU.mult)
                ve.tensor_tensor(dg, L[:, :, 0:NG], wide(gtop, NG), ALU.subtract).then_inc(s_dg, 1)
                then(ins)
                then(ve.tensor_tensor(M, M, L[:, :, NG:NR], ALU.add))
                first_max(M, NE, v1, hit, idx1)
                then(ve.tensor_tensor(one1, numbers(NE), wide(idx1, NE), ALU.is_equal))
                then(ve.scalar_tensor_tensor(M, one1, -3 * PEN, M, ALU.mult, ALU.add))
                first_max(M, NE, v2, hit, idx2)
                for t in range(TH):
                    ins = ve.scalar_tensor_tensor(A[:, t, :], places, idx2[:, t:t + 1], one1[:, t, :], ALU.is_equal, ALU.add)
                ins.then_inc(s_A, 1)
                ve.tensor_tensor(d2, v2, v1, ALU.subtract).then_inc(s_dg, 1)
                then(ve.tensor_tensor(one2, numbers(NE), wide(idx2, NE), ALU.is_equal))
                ve.wait_ge(s_rk, layer + 1)
                then(ve.scalar_tensor_tensor(R[:, :, 0:NE], ps[:, 6, 0:2 * NE].rearrange("p (t e) -> p t e", t=TH), 1.0,
                                             A[:, :, :], ALU.add, ALU.mult))
                place(main, 0)
                counts, most = sm(640, NE), sm(640 + NE, NGRP)
                then(ve.tensor_copy(counts, ps[:, 6, 2 * NE:3 * NE]))
                then(ve.tensor_reduce(most, counts.rearrange("p (g e) -> p g e", g=NGRP), AX, ALU.max))
                then(ve.tensor_reduce(sm(640 + NE + NGRP, 1), most, AX, ALU.max))
                then(ve.tensor_copy(cnt[:, :], sm(640, NE + NGRP + 1)))
                if layer == 0:
                    then(ve.memset(ps[:, 5:8, :], 0.0))
                ve.sem_inc(s_route, 1)

            def gates(layer):
                eg, e2 = sm(400, TH, NG), sm(416, TH)
                gs, den, w1, w2 = sm(486, TH), sm(490, TH), sm(492, TH), sm(494, TH)
                one1, one2 = sm(512, TH, NE), sm(576, TH, NE)
                ve.wait_ge(s_eg, 2 * layer + 1)
                then(ve.tensor_reduce(gs, eg, AX, ALU.add))
                ve.wait_ge(s_eg, 2 * layer + 2)
                then(ve.tensor_scalar(den, e2, 1.0, None, ALU.add))
                then(ve.tensor_tensor(den, den, gs, ALU.mult))
                then(ve.reciprocal(w1, den))
                then(ve.tensor_tensor(w2, w1, e2, ALU.mult))
                then(ve.tensor_tensor(one1, one1, wide(w1, NE), ALU.mult))
                then(ve.tensor_tensor(one2, one2, wide(w2, NE), ALU.mult))
                then(ve.tensor_tensor(W[:, :, :], one1, one2, ALU.add))

            def place(s, gl):
                for t in range(TH):
                    ins = ve.tensor_tensor(onehot[:, t, :, :, :],
                                           iota.rearrange("p (b s) -> p b s", b=NB).unsqueeze(2).to_broadcast([P, NB, E4, SB]),
                                           R[:, t, bass.ds(gl * E4, E4)].unsqueeze(1).unsqueeze(3).to_broadcast([P, NB, E4, SB]),
                                           ALU.is_equal)
                ins.then_inc(s["onehot"], 1)

            def gate_rows(s, n1, blocks):
                b = slice(0, blocks)
                ve.wait_ge(s["exp"], n1)
                ve.tensor_scalar(sg[:, 1, b, :], sg[:, 0, b, :], 1.0, None, ALU.add).then_inc(s["den"], 1)
                ve.wait_ge(s["den"], n1)
                ve.reciprocal(sg[:, 2, b, :], sg[:, 1, b, :]).then_inc(s["sig"], 1)
                ve.wait_ge(s["sig"], n1)
                ve.tensor_tensor(sg[:, 3, b, :], sg[:, 2, b, :], gu_ps[:, b, 0, :], ALU.mult).then_inc(s["gh"], 1)
                ve.wait_ge(s["gh"], n1)
                ve.tensor_tensor(act[:, b, :], sg[:, 3, b, :], gu_ps[:, b, 1, :], ALU.mult).then_inc(s["act"], 1)

            def group(s, g, gl, placed, tokens):
                ve.wait_ge(s["onehot"], placed)
                for t in range(TH):
                    ins = ve.tensor_tensor(gated[:, t, :, :, :], onehot[:, t, :, :, :],
                                           W[:, t, bass.ds(gl * E4, E4)].unsqueeze(1).unsqueeze(3).to_broadcast([P, NB, E4, SB]),
                                           ALU.mult)
                ins.then_inc(s["gated"], 1)
                for k in range(E4):
                    n1 = g * E4 + (k + 1)
                    count = tokens(k)
                    if count is None:
                        gate_rows(s, n1, NB)
                    else:
                        with ve.If(count > SB):
                            gate_rows(s, n1, NB)
                        with ve.Else():
                            gate_rows(s, n1, 1)
                    ve.wait_ge(s["at"], n1)
                    ve.tensor_copy(actT[:, :, :], at_ps).then_inc(s["atc"], 1)
                    ve.wait_ge(s["y"], n1)
                    for i in (0, 1):
                        ins = ve.tensor_copy(y[SB * k:SB * (k + 1), :, 256 * i:256 * (i + 1)],
                                             y_ps[SB * i:SB * (i + 1), :, :])
                    ins.then_inc(s["yc_v"], 1)
                place(s, gl + 1)

            def experts(layer):
                gates(layer)
                with ve.Fori(0, NGRP) as g:
                    def tokens(k):
                        return ve.value_load(cnt[0:1, bass.ds(g * E4 + k, 1)], min_val=0, max_val=S)

                    group(main, g + layer * NGRP, g, g + (layer * (NGRP + 1) + 1), tokens)
                fb = more[layer]
                most = ve.value_load(cnt[0:1, NE + NGRP:NE + NGRP + 1], min_val=0, max_val=S)
                with ve.If(most > CAP):
                    with ve.Fori(0, PASSES - 1) as m:
                        with ve.If(most > CAP * m + CAP):
                            ve.tensor_scalar(R[:, :, 0:NE], R[:, :, 0:NE], -float(CAP), None, ALU.add).then_inc(fb["shift"], 1)
                            ve.wait_ge(fb["shift"], m + 1)
                            place(fb, 0)
                            with ve.Fori(0, NGRP) as g:
                                group(fb, m * NGRP + g, g, m * (NGRP + 1) + g + 1, lambda k: None)
                                ve.wait_ge(fb["sc"], ACC * (m * NGRP + g + 1))

            def residual(t, done, before):
                for i in range(2):
                    ve.wait_ge(done, before + 2 * t + i + 1)
                    xs = x_sb[:, t, 512 * i:512 * (i + 1)]
                    ins = ve.tensor_tensor(xs, xs, ps[:, 2 * t + i, :], ALU.add)
                ins.then_inc(s_x2, 1)

            ve.memset(ones_row, 1.0)
            ve.memset(eps_x, RMS_EPS)
            ve.memset(eps_o, SUB_EPS)
            then(ve.memset(R[:, :, NE:NE + E4], 0.0))
            ve.memset(zero, 0.0).then_inc(s_z, 1)
            ve.wait_ge(s_bc, 1)
            for t in range(TH):
                ve.wait_ge(s_x[t], 16)
                norm(0, t, ps[:, 4:6, :].rearrange("p a b -> p (a b)"), False)
            for g in (0, 2):
                ve.wait_ge(s_mix, g + 1)
                ve.tensor_copy(mixT[:, 2 * g:2 * g + 2, :], ps[:, g, :].rearrange("p (m s) -> p m s", m=2))\
                  .then_inc(s_mixT[0], 1)
            ve.wait_ge(s_bcc, 1)
            for t in range(TH):
                ve.wait_ge(s_po, t + 1)
                then(ve.tensor_tensor(h_sb[:, t, :], gain[:, 1, :], ps[:, 4 + 2 * t:6 + 2 * t, :].rearrange("p a b -> p (a b)"),
                                      ALU.mult))
                ve.tensor_tensor(x_sb[:, t, :], x_sb[:, t, :], h_sb[:, t, :], ALU.add).then_inc(s_x2, 1)
                if t == 0:
                    ve.wait_ge(s_bcc, 2)
                router_norm(1, t, ffn0)
                copy_hT(0, t)
            ve.wait_ge(s_c, 16)
            route(0)
            experts(0)

            ve.wait_ge(s_bcc, 3)
            for t in range(TH):
                residual(t, main["sc"], ACC * (NGRP - 1))
                norm(2, t, gain[:, 0, :], True)
                copy_hT(1, t)
            ve.wait_ge(s_lam, 80)
            for i in range(2):
                then(ve.tensor_tensor(small[:, 700:764], lam4[:, 2 * i, :], lam4[:, 2 * i + 1, :], ALU.mult))
                then(ve.tensor_reduce(small[:, 432 + i:433 + i], small[:, 700:764], AX, ALU.add))
            ve.sem_inc(s_ls, 1)
            ve.wait_ge(s_le, 1)
            lam = small[:, 436:437]
            then(ve.tensor_tensor(lam, small[:, 434:435], small[:, 435:436], ALU.subtract))
            then(ve.tensor_scalar(lam, lam, LAM_INIT, None, ALU.add))
            then(ve.tensor_scalar(subg[:, :], subg[:, :], 1.0 - LAM_INIT, None, ALU.mult))
            for t in range(TH):
                ve.wait_ge(s_vp, t + 1)
                ve.tensor_copy(v_sb[:, t, 512:1024], ps[:, 2 * t + 1, :]).then_inc(s_vs[0], 1)

            def logits(h):
                ve.wait_ge(s_S, h + 1)
                for c in range(2):
                    ve.scalar_tensor_tensor(prob[:, h % 2, c, :], dist, -(2.0 ** (-8.0 * (h + 1) / NH)),
                                            ps[:, 2 + c, 0:LW], ALU.mult, ALU.add).then_inc(s_L, 1)
                ve.wait_ge(s_L, 2 * (h + 1))
                for c in range(2):
                    for t, cols in ((0, slice(0, P)), (1, slice(P, LW))):
                        at = 440 + 8 * (h % 2) + 2 * c + t
                        ve.tensor_reduce(small[:, at:at + 1], prob[:, h % 2, c, cols], AX, ALU.max, negate=True)\
                          .then_inc(s_m, 1)

            def weights(h):
                ve.wait_ge(s_ex, 4 * (h + 1))
                at = 444 + 8 * (h % 2)
                r = small[:, 770:774]
                then(ve.reciprocal(r, small[:, at:at + 4]))
                then(ve.tensor_scalar(r[:, 2:4], r[:, 2:4], lam, None, ALU.mult))
                for t, cols in ((0, slice(0, P)), (1, slice(P, LW))):
                    ins = ve.tensor_scalar(prob[:, h % 2, 1, cols], prob[:, h % 2, 1, cols], r[:, 2 + t:3 + t], None, ALU.mult)
                then(ins)
                ve.scalar_tensor_tensor(kT[:, h, 0:P], prob[:, h % 2, 0, 0:P], r[:, 0:1], prob[:, h % 2, 1, 0:P],
                                        ALU.mult, ALU.subtract)
                then(ve.scalar_tensor_tensor(qT[:, h, :], prob[:, h % 2, 0, P:LW], r[:, 1:2], prob[:, h % 2, 1, P:LW],
                                             ALU.mult, ALU.subtract))
                ve.sem_inc(s_p, 1)

            def normalise(h):
                ve.wait_ge(s_osq, h + 1)
                then(ve.tensor_scalar(mean_o, small[:, 460:462], -0.5 / (2 * HD), -0.5 * SUB_EPS, ALU.mult, ALU.add))
                ve.wait_ge(s_oroot, h + 1)
                newton(small[:, 464:466], mean_o, newt_o)
                for t in range(TH):
                    ins = ve.scalar_tensor_tensor(h_sb[:, t, h * P:(h + 1) * P], ps[:, 5 + h % 2, t * P:(t + 1) * P],
                                                  small[:, 464 + t:465 + t], subg[:, :], ALU.mult, ALU.mult)
                ins.then_inc(s_os, 1)

            for h in range(1, NH + 3):
                if h <= NH:
                    logits(h - 1)
                if 3 <= h:
                    normalise(h - 3)
                if h <= NH:
                    weights(h - 1)
            ve.wait_ge(gain_in[1], 16)
            for t in range(TH):
                residual(t, s_wo, 0)
                router_norm(3, t, gain[:, 1, :])
                copy_hT(2, t)
            route(1)
            experts(1)
            ve.wait_ge(gain_in[0], 16)
            for t in range(TH):
                residual(t, main["sc"], ACC * (2 * NGRP - 1))
            for t in range(TH):
                norm(4, t, gain[:, 0, :], False)


_INS = ["x", "norm_mix_g", "norm_ffn_g", "pool_w", "pool_scale", "attn_wq", "attn_wk", "attn_wv", "attn_wo",
        "attn_lq1", "attn_lk1", "attn_lq2", "attn_lk2", "attn_subln_g", "moe_wg", "moe_bg", "moe_we", "moe_be",
        "moe_w1", "moe_w3", "moe_w2", "final_g"]


def kernel(**inputs):
    import concourse.bacc as bacc
    from concourse.bass_utils import run_bass_kernel_spmd

    nc = bacc.Bacc("TRN2", target_bir_lowering=False, num_devices=1)
    arrays, args = {}, []
    for name in _INS + ["consts"]:
        a = shape_constants() if name == "consts" else np.ascontiguousarray(inputs[name])
        arrays[f"in_{name}"] = a
        args.append(nc.dram_tensor(f"in_{name}", a.shape, mybir.dt.from_np(a.dtype), kind="ExternalInput").ap())
    args.append(nc.dram_tensor("out_x", (1, S, D), F32, kind="ExternalOutput").ap())
    build(nc, *args)
    r = run_bass_kernel_spmd(nc, [arrays], core_ids=[0])
    return r.results[0]["out_x"]
```
